# Optimizing a Trainium2 kernel written in Bass

```python
import math
import jax, jax.numpy as jnp
from jax import lax
import numpy as np

D_MODEL = 1024
BATCH = 1
SEQ = 256
DEPTH = 2

HEAD_DIM = 64
RET_HEADS = 4
RET_DK = 64
RET_DV = 128
DIL_HEADS = 4
SB_HEADS = 4
MIX_WIDTH = RET_HEADS * RET_DV + DIL_HEADS * HEAD_DIM + SB_HEADS * HEAD_DIM
IN_SIZES = (RET_HEADS * RET_DK, RET_HEADS * RET_DK, RET_HEADS * RET_DV, RET_HEADS * RET_DV,
            DIL_HEADS * HEAD_DIM, DIL_HEADS * HEAD_DIM, DIL_HEADS * HEAD_DIM,
            SB_HEADS * HEAD_DIM, SB_HEADS * HEAD_DIM, SB_HEADS * HEAD_DIM)
IN_WIDTH = sum(IN_SIZES)
D_FF = 2816
BLOCK = 128
RET_CHUNK = 128
WINDOWS = (128, 512, 2048)
DILATIONS = (1, 4, 16)
ROPE_THETA = 10000.0
ALPHA = (2.0 * DEPTH) ** 0.25
BETA = (8.0 * DEPTH) ** -0.25
LN_EPS = 1e-5
GN_EPS = 1e-6
FFN_RES = 0.5
N_MOD = 9


def _layer_norm(x, gain, bias):
    xf = x.astype(jnp.float32)
    mu = jnp.mean(xf, -1, keepdims=True)
    var = jnp.mean(jnp.square(xf - mu), -1, keepdims=True)
    y = (xf - mu) * lax.rsqrt(var + LN_EPS)
    return (y * gain.astype(jnp.float32) + bias.astype(jnp.float32)).astype(x.dtype)

def _modulate(x, shift, scale):
    return x * (1.0 + scale) + shift

def _post_norm(x, y, gate, res_w, gain, bias):
    return _layer_norm(ALPHA * x + res_w * (1.0 + gate) * y, gain, bias)

def _swiglu(h, w_gate, w_up, w_down):
    return (jax.nn.silu(h @ w_gate) * (h @ w_up)) @ w_down

def _split_heads(x, n_heads):
    b, s, _ = x.shape
    return x.reshape(b, s, n_heads, -1).transpose(0, 2, 1, 3)

def _merge_heads(x):
    b, h, s, d = x.shape
    return x.transpose(0, 2, 1, 3).reshape(b, s, h * d)

def _rotate(x, inv_freq):
    s, d = x.shape[2], x.shape[3]
    ang = jnp.arange(s, dtype=jnp.float32)[:, None] * inv_freq[None, :]
    cos, sin = jnp.cos(ang), jnp.sin(ang)
    xf = x.astype(jnp.float32)
    x1, x2 = xf[..., : d // 2], xf[..., d // 2:]
    return jnp.concatenate([x1 * cos - x2 * sin, x1 * sin + x2 * cos], -1).astype(x.dtype)

def _retention(q, k, v, g):
    b, h, s, dk = q.shape
    dv = v.shape[-1]
    c = RET_CHUNK
    n = s // c
    log_gamma = jnp.log1p(-jnp.exp2(-5.0 - jnp.arange(h, dtype=jnp.float32)))
    i = jnp.arange(c, dtype=jnp.float32)
    diff = i[:, None] - i[None, :]
    decay_in = jnp.where(diff >= 0, jnp.exp(log_gamma[:, None, None] * jnp.maximum(diff, 0.0)), 0.0)
    xi = jnp.exp(log_gamma[:, None] * (i + 1.0))
    zeta = jnp.exp(log_gamma[:, None] * (c - 1.0 - i))
    gamma_c = jnp.exp(log_gamma * c)
    qc = q.astype(jnp.float32).reshape(b, h, n, c, dk)
    kc = (k.astype(jnp.float32) * dk ** -0.5).reshape(b, h, n, c, dk)
    vc = v.astype(jnp.float32).reshape(b, h, n, c, dv)
    scores = jnp.einsum('bhncd,bhnmd->bhncm', qc, kc) * decay_in[None, :, None]
    o_inner = jnp.einsum('bhncm,bhnme->bhnce', scores, vc)
    kv = jnp.einsum('bhncd,bhnce->bhnde', kc * zeta[None, :, None, :, None], vc)

    def step(state, kv_n):
        return state * gamma_c[None, :, None, None] + kv_n, state

    init = jnp.zeros((b, h, dk, dv), jnp.float32)
    _, prev = lax.scan(step, init, jnp.moveaxis(kv, 2, 0))
    prev = jnp.moveaxis(prev, 0, 2)
    o_cross = jnp.einsum('bhncd,bhnde->bhnce', qc, prev) * xi[None, :, None, :, None]
    o = (o_inner + o_cross).reshape(b, h, s, dv)
    mu = jnp.mean(o, -1, keepdims=True)
    var = jnp.mean(jnp.square(o - mu), -1, keepdims=True)
    o = (o - mu) * lax.rsqrt(var + GN_EPS)
    return jax.nn.silu(g.astype(jnp.float32)) * _merge_heads(o)

def _dilated_attention(q, k, v):
    b, h, s, d = q.shape
    nb = s // BLOCK
    n_keys = max(w // dl for w, dl in zip(WINDOWS, DILATIONS)) + 1
    dist = jnp.array(DILATIONS, jnp.int32)[:, None] * jnp.arange(n_keys, dtype=jnp.int32)[None, :]
    in_win = dist <= jnp.array(WINDOWS, jnp.int32)[:, None]
    qb = (q.astype(jnp.float32) * d ** -0.5).reshape(b, h, nb, BLOCK, d).transpose(2, 0, 1, 3, 4)
    kf = k.astype(jnp.float32)
    vf = v.astype(jnp.float32)

    def block(args):
        q_blk, start = args
        t = start + jnp.arange(BLOCK, dtype=jnp.int32)
        idx = t[:, None, None] - dist[None]
        valid = (idx >= 0) & in_win[None]
        idx = jnp.maximum(idx, 0)
        k_g = jnp.take(kf, idx, axis=2)
        v_g = jnp.take(vf, idx, axis=2)
        sc = jnp.einsum('bhqd,bhqpjd->bhqpj', q_blk, k_g)
        sc = jnp.where(valid, sc, -jnp.inf)
        m = jnp.max(sc, -1)
        e = jnp.exp(sc - m[..., None])
        den = jnp.sum(e, -1)
        o_p = jnp.einsum('bhqpj,bhqpjd->bhqpd', e, v_g) / den[..., None]
        wgt = den * jnp.exp(m - jnp.max(m, -1, keepdims=True))
        wgt = wgt / jnp.sum(wgt, -1, keepdims=True)
        return jnp.einsum('bhqp,bhqpd->bhqd', wgt, o_p)

    out = lax.map(block, (qb, jnp.arange(nb, dtype=jnp.int32) * BLOCK))
    return out.transpose(1, 2, 0, 3, 4).reshape(b, h, s, d)

def _stick_breaking(q, k, v):
    b, h, s, d = q.shape
    nb = s // BLOCK
    qb = (q.astype(jnp.float32) * d ** -0.5).reshape(b, h, nb, BLOCK, d).transpose(2, 0, 1, 3, 4)
    kf = k.astype(jnp.float32)
    vf = v.astype(jnp.float32)
    key_pos = jnp.arange(s, dtype=jnp.int32)

    def block(args):
        q_blk, start = args
        t = start + jnp.arange(BLOCK, dtype=jnp.int32)
        z = jnp.einsum('bhqd,bhsd->bhqs', q_blk, kf)
        causal = key_pos[None, :] < t[:, None]
        log_beta = jax.nn.log_sigmoid(z)
        log_keep = jnp.where(causal, jax.nn.log_sigmoid(-z), 0.0)
        between = lax.cumsum(log_keep, axis=3, reverse=True) - log_keep
        a = jnp.where(causal, jnp.exp(log_beta + between), 0.0)
        return jnp.einsum('bhqs,bhsd->bhqd', a, vf)

    out = lax.map(block, (qb, jnp.arange(nb, dtype=jnp.int32) * BLOCK))
    return out.transpose(1, 2, 0, 3, 4).reshape(b, h, s, d)

def _token_mixer(h, w_in, w_out):
    proj = h @ w_in
    points, acc = [], 0
    for size in IN_SIZES[:-1]:
        acc += size
        points.append(acc)
    rq, rk, rv, rg, dq, dk, dv, sq, sk, sv = jnp.split(proj, points, axis=-1)
    ret_freq = 1.0 / (ROPE_THETA ** jnp.linspace(0.0, 1.0, RET_DK // 2, dtype=jnp.float32))
    rope_freq = 1.0 / (ROPE_THETA ** (jnp.arange(0, HEAD_DIM, 2, dtype=jnp.float32) / HEAD_DIM))
    y_ret = _retention(_rotate(_split_heads(rq, RET_HEADS), ret_freq),
                       _rotate(_split_heads(rk, RET_HEADS), ret_freq),
                       _split_heads(rv, RET_HEADS), rg)
    y_dil = _merge_heads(_dilated_attention(_rotate(_split_heads(dq, DIL_HEADS), rope_freq),
                                            _rotate(_split_heads(dk, DIL_HEADS), rope_freq),
                                            _split_heads(dv, DIL_HEADS)))
    y_sb = _merge_heads(_stick_breaking(_split_heads(sq, SB_HEADS), _split_heads(sk, SB_HEADS),
                                        _split_heads(sv, SB_HEADS)))
    y = jnp.concatenate([y_ret, y_dil, y_sb], -1).astype(h.dtype)
    return y @ w_out

def first_inputs(seed: int = 0) -> dict:
    key = jax.random.key(seed)
    ks = jax.random.split(key, 16)
    f32 = jnp.float32
    nrm = lambda k, shape, scale: jax.random.normal(k, shape, f32) * scale
    return {
        'x': nrm(ks[0], (BATCH, SEQ, D_MODEL), 1.0),
        'c': nrm(ks[1], (BATCH, D_MODEL), 1.0),
        'w_ada': nrm(ks[2], (DEPTH, D_MODEL, N_MOD * D_MODEL), 0.3 * D_MODEL ** -0.5),
        'b_ada': nrm(ks[3], (DEPTH, N_MOD * D_MODEL), 0.01),
        'ln_gain': 1.0 + nrm(ks[4], (DEPTH, 3, D_MODEL), 0.01),
        'ln_bias': nrm(ks[5], (DEPTH, 3, D_MODEL), 0.01),
        'ffn1_w_gate': nrm(ks[6], (DEPTH, D_MODEL, D_FF), D_MODEL ** -0.5),
        'ffn1_w_up': nrm(ks[7], (DEPTH, D_MODEL, D_FF), D_MODEL ** -0.5),
        'ffn1_w_down': nrm(ks[8], (DEPTH, D_FF, D_MODEL), BETA * D_FF ** -0.5),
        'w_in': nrm(ks[9], (DEPTH, D_MODEL, IN_WIDTH), D_MODEL ** -0.5),
        'w_out': nrm(ks[10], (DEPTH, MIX_WIDTH, D_MODEL), BETA * MIX_WIDTH ** -0.5),
        'ffn2_w_gate': nrm(ks[11], (DEPTH, D_MODEL, D_FF), D_MODEL ** -0.5),
        'ffn2_w_up': nrm(ks[12], (DEPTH, D_MODEL, D_FF), D_MODEL ** -0.5),
        'ffn2_w_down': nrm(ks[13], (DEPTH, D_FF, D_MODEL), BETA * D_FF ** -0.5),
    }

def first_block(x, c, w_ada, b_ada, ln_gain, ln_bias, ffn1_w_gate, ffn1_w_up, ffn1_w_down,
              w_in, w_out, ffn2_w_gate, ffn2_w_up, ffn2_w_down):
    cond = jax.nn.silu(c)
    for l in range(DEPTH):
        mod = cond @ w_ada[l] + b_ada[l]
        sh1, sc1, g1, sh2, sc2, g2, sh3, sc3, g3 = jnp.split(mod[:, None, :].astype(x.dtype), N_MOD, axis=-1)
        y = _swiglu(_modulate(x, sh1, sc1), ffn1_w_gate[l], ffn1_w_up[l], ffn1_w_down[l])
        x = _post_norm(x, y, g1, FFN_RES, ln_gain[l, 0], ln_bias[l, 0])
        y = _token_mixer(_modulate(x, sh2, sc2), w_in[l], w_out[l])
        x = _post_norm(x, y, g2, 1.0, ln_gain[l, 1], ln_bias[l, 1])
        y = _swiglu(_modulate(x, sh3, sc3), ffn2_w_gate[l], ffn2_w_up[l], ffn2_w_down[l])
        x = _post_norm(x, y, g3, FFN_RES, ln_gain[l, 2], ln_bias[l, 2])
    return x


GRID_W = 64
CTX_LEN = 256
N_Q_HEADS = 8
N_KV_HEADS = 2
ATTN_WIDTH = N_Q_HEADS * HEAD_DIM
KV_WIDTH = N_KV_HEADS * HEAD_DIM
Q_BLOCK = 128
POOL_WINDOWS = (2, 4, 8, 16)
N_POOL_GROUPS = 4
POOL_GROUP_DIM = 128
POOL_WIDTH = N_POOL_GROUPS * POOL_GROUP_DIM
MIX_IN_WIDTH = ATTN_WIDTH + 2 * KV_WIDTH + POOL_WIDTH
MIX_OUT_WIDTH = ATTN_WIDTH + POOL_WIDTH
CONV_WIDTH = D_MODEL
CONV_K = 3
N_EXPERTS = 16
EXPERT_FF = 1024
CAPACITY_FACTOR = 2
NORM_EPS = 1e-6
DEEPNORM_ALPHA = (2 * DEPTH) ** 0.25
DEEPNORM_BETA = (8 * DEPTH) ** -0.25


def _layer_norm_2(x, g, b):
    xf = x.astype(jnp.float32)
    mu = jnp.mean(xf, axis=-1, keepdims=True)
    xc = xf - mu
    var = jnp.mean(xc * xc, axis=-1, keepdims=True)
    y = xc * lax.rsqrt(var + NORM_EPS) * g.astype(jnp.float32) + b.astype(jnp.float32)
    return y.astype(x.dtype)

def _rms_norm(x, g):
    xf = x.astype(jnp.float32)
    y = xf * lax.rsqrt(jnp.mean(xf * xf, axis=-1, keepdims=True) + NORM_EPS)
    return (y * g.astype(jnp.float32)).astype(x.dtype)

def _modulation(cond, w, b):
    m = (cond @ w + b)[:, None, :]
    return jnp.split(m, 6, axis=-1)

def _modulate_2(h, shift, scale):
    return h * (1.0 + scale) + shift

def _post_norm_2(h, branch, g, b):
    return _layer_norm_2(DEEPNORM_ALPHA * h + branch, g, b)

def _axial_rope_tables(rows):
    row = jnp.broadcast_to(jnp.arange(rows, dtype=jnp.float32)[:, None], (rows, GRID_W)).reshape(-1)
    col = jnp.broadcast_to(jnp.arange(GRID_W, dtype=jnp.float32)[None, :], (rows, GRID_W)).reshape(-1)
    axis_dim = HEAD_DIM // 2
    inv_freq = ROPE_THETA ** (-jnp.arange(0, axis_dim, 2, dtype=jnp.float32) / axis_dim)
    ang = jnp.concatenate([row[:, None] * inv_freq, col[:, None] * inv_freq], axis=-1)
    return jnp.cos(ang), jnp.sin(ang)

def _apply_rope(x, cos, sin):
    xf = x.astype(jnp.float32).reshape(x.shape[:-1] + (HEAD_DIM // 2, 2))
    x0, x1 = xf[..., 0], xf[..., 1]
    c = cos[None, :, None, :]
    s = sin[None, :, None, :]
    out = jnp.stack([x0 * c - x1 * s, x0 * s + x1 * c], axis=-1).reshape(x.shape)
    return out.astype(x.dtype)

def _blocked_attention(q, k, v):
    b, lq = q.shape[:2]
    grp = N_Q_HEADS // N_KV_HEADS
    nb = lq // Q_BLOCK
    qb = q.reshape(b, nb, Q_BLOCK, N_KV_HEADS, grp, HEAD_DIM).transpose(1, 0, 2, 3, 4, 5)
    scale = HEAD_DIM ** -0.5

    def one_block(qi):
        s = jnp.einsum('bqhgd,bkhd->bhgqk', qi, k, preferred_element_type=jnp.float32) * scale
        p = jax.nn.softmax(s, axis=-1)
        return jnp.einsum('bhgqk,bkhd->bqhgd', p.astype(v.dtype), v)

    o = lax.map(one_block, qb)
    return o.transpose(1, 0, 2, 3, 4, 5).reshape(b, lq, ATTN_WIDTH)

def _pool_branch(p, w_grp, p_scale):
    b, l, _ = p.shape
    pf = p.astype(jnp.float32)
    cs = jnp.concatenate([jnp.zeros((b, 1, POOL_WIDTH), jnp.float32), jnp.cumsum(pf, axis=1)], axis=1)
    t = jnp.arange(l)
    means = []
    for g, w in enumerate(POOL_WINDOWS):
        lo = jnp.maximum(t - w // 2, 0)
        hi = jnp.minimum(t + w // 2, l)
        seg = cs[:, :, g * POOL_GROUP_DIM:(g + 1) * POOL_GROUP_DIM]
        cnt = (hi - lo).astype(jnp.float32)[None, :, None]
        means.append((seg[:, hi] - seg[:, lo]) / cnt)
    pooled = (jnp.concatenate(means, axis=-1) - pf).astype(p.dtype)
    pooled = pooled.reshape(b, l, N_POOL_GROUPS, POOL_GROUP_DIM)
    out = jnp.einsum('blgc,gcd->blgd', pooled, w_grp).reshape(b, l, POOL_WIDTH)
    return out * p_scale

def _split_mix_in(h):
    return jnp.split(h, [ATTN_WIDTH, ATTN_WIDTH + KV_WIDTH, ATTN_WIDTH + 2 * KV_WIDTH], axis=-1)

def _attn_pool_mixer(u_lat, u_ctx, cos, sin, w_in, q_g, k_g, w_grp, p_scale, w_out, ctx_out):
    b, s, _ = u_lat.shape
    lc = u_ctx.shape[1]
    q, k, v, p = _split_mix_in(u_lat @ w_in)
    q = _apply_rope(_rms_norm(q.reshape(b, s, N_Q_HEADS, HEAD_DIM), q_g), cos, sin)
    k = _apply_rope(_rms_norm(k.reshape(b, s, N_KV_HEADS, HEAD_DIM), k_g), cos, sin)
    v = v.reshape(b, s, N_KV_HEADS, HEAD_DIM)
    if ctx_out:
        qc, kc, vc, pc = _split_mix_in(u_ctx @ w_in)
    else:
        kc, vc = jnp.split(u_ctx @ w_in[:, ATTN_WIDTH:ATTN_WIDTH + 2 * KV_WIDTH], 2, axis=-1)
    kc = _rms_norm(kc.reshape(b, lc, N_KV_HEADS, HEAD_DIM), k_g)
    vc = vc.reshape(b, lc, N_KV_HEADS, HEAD_DIM)
    k_all = jnp.concatenate([kc, k], axis=1)
    v_all = jnp.concatenate([vc, v], axis=1)
    a_lat = _blocked_attention(q, k_all, v_all)
    y_lat = jnp.concatenate([a_lat, _pool_branch(p, w_grp, p_scale)], axis=-1) @ w_out
    y_ctx = None
    if ctx_out:
        qc = _rms_norm(qc.reshape(b, lc, N_Q_HEADS, HEAD_DIM), q_g)
        a_ctx = _blocked_attention(qc, kc, vc)
        y_ctx = jnp.concatenate([a_ctx, _pool_branch(pc, w_grp, p_scale)], axis=-1) @ w_out
    return y_lat, y_ctx

def _short_conv_mixer(u, w_in, conv_w, w_out):
    b_gate, c_gate, x_in = jnp.split(u @ w_in, 3, axis=-1)
    z = lax.conv_general_dilated(c_gate * x_in, conv_w[:, None, :], window_strides=(1,),
                                 padding=((CONV_K // 2, CONV_K // 2),),
                                 dimension_numbers=('NWC', 'WIO', 'NWC'),
                                 feature_group_count=CONV_WIDTH)
    return (b_gate * z) @ w_out

def _expert_choice_ffn(u, w_router, w_g, w_u, w_d):
    b, n, _ = u.shape
    cap = CAPACITY_FACTOR * n // N_EXPERTS
    logits = jnp.einsum('bnd,de->ben', u, w_router, preferred_element_type=jnp.float32)
    aff = jax.nn.softmax(logits, axis=1)
    gate, idx = lax.top_k(aff, cap)
    bidx = jnp.arange(b)[:, None, None]
    xe = u[bidx, idx]
    hg = jnp.einsum('becd,edf->becf', xe, w_g)
    hu = jnp.einsum('becd,edf->becf', xe, w_u)
    ye = jnp.einsum('becf,efd->becd', jax.nn.silu(hg) * hu, w_d) * gate[..., None].astype(u.dtype)
    return jnp.zeros_like(u).at[bidx, idx].add(ye)

def second_inputs(seed: int = 0) -> dict:
    key = jax.random.key(seed)
    ks = jax.random.split(key, 24)
    f32 = jnp.float32
    n_even = (DEPTH + 1) // 2
    n_odd = DEPTH // 2

    def dense(k, shape, fan_in, mult=1.0):
        return jax.random.normal(k, shape, f32) * (mult * fan_in ** -0.5)

    def gain(k, shape):
        return 1.0 + 0.02 * jax.random.normal(k, shape, f32)

    def small(k, shape):
        return 0.02 * jax.random.normal(k, shape, f32)

    return {
        'x': jax.random.normal(ks[0], (BATCH, SEQ, D_MODEL), f32),
        'c': jax.random.normal(ks[1], (BATCH, D_MODEL), f32),
        'ctx': jax.random.normal(ks[2], (BATCH, CTX_LEN, D_MODEL), f32),
        'c_ctx': jax.random.normal(ks[3], (D_MODEL,), f32),
        'w_mod': dense(ks[4], (DEPTH, D_MODEL, 6 * D_MODEL), D_MODEL, 0.5),
        'b_mod': 0.01 * jax.random.normal(ks[5], (DEPTH, 6 * D_MODEL), f32),
        'ln_mix_g': gain(ks[6], (DEPTH, D_MODEL)),
        'ln_mix_b': small(ks[7], (DEPTH, D_MODEL)),
        'ln_ffn_g': gain(ks[8], (DEPTH, D_MODEL)),
        'ln_ffn_b': small(ks[9], (DEPTH, D_MODEL)),
        'w_mix_in': dense(ks[10], (n_even, D_MODEL, MIX_IN_WIDTH), D_MODEL),
        'q_norm_g': gain(ks[11], (n_even, HEAD_DIM)),
        'k_norm_g': gain(ks[12], (n_even, HEAD_DIM)),
        'w_pool_grp': dense(ks[13], (n_even, N_POOL_GROUPS, POOL_GROUP_DIM, POOL_GROUP_DIM), POOL_GROUP_DIM),
        'pool_scale': gain(ks[14], (n_even, POOL_WIDTH)),
        'w_mix_out': dense(ks[15], (n_even, MIX_OUT_WIDTH, D_MODEL), MIX_OUT_WIDTH, DEEPNORM_BETA),
        'w_conv_in': dense(ks[16], (n_odd, D_MODEL, 3 * CONV_WIDTH), D_MODEL),
        'conv_w': dense(ks[17], (n_odd, CONV_K, CONV_WIDTH), CONV_K),
        'w_conv_out': dense(ks[18], (n_odd, CONV_WIDTH, D_MODEL), CONV_WIDTH, DEEPNORM_BETA),
        'w_router': dense(ks[19], (DEPTH, D_MODEL, N_EXPERTS), D_MODEL),
        'w_exp_gate': dense(ks[20], (DEPTH, N_EXPERTS, D_MODEL, EXPERT_FF), D_MODEL),
        'w_exp_up': dense(ks[21], (DEPTH, N_EXPERTS, D_MODEL, EXPERT_FF), D_MODEL),
        'w_exp_down': dense(ks[22], (DEPTH, N_EXPERTS, EXPERT_FF, D_MODEL), EXPERT_FF, DEEPNORM_BETA),
    }

def second_block(x, c, ctx, c_ctx, w_mod, b_mod, ln_mix_g, ln_mix_b, ln_ffn_g, ln_ffn_b,
              w_mix_in, q_norm_g, k_norm_g, w_pool_grp, pool_scale, w_mix_out,
              w_conv_in, conv_w, w_conv_out,
              w_router, w_exp_gate, w_exp_up, w_exp_down):
    rows = x.shape[1] // GRID_W
    cos, sin = _axial_rope_tables(rows)
    cond_lat = jax.nn.silu(c)
    cond_ctx = jax.nn.silu(c_ctx)[None, :]
    h_lat, h_ctx = x, ctx
    for layer in range(DEPTH):
        is_even = layer % 2 == 0
        ctx_out = any(j % 2 == 0 for j in range(layer + 1, DEPTH))
        ctx_in = is_even or ctx_out
        m_lat = _modulation(cond_lat, w_mod[layer], b_mod[layer])
        u_lat = _modulate_2(h_lat, m_lat[0], m_lat[1])
        u_ctx = None
        if ctx_in:
            m_ctx = _modulation(cond_ctx, w_mod[layer], b_mod[layer])
            u_ctx = _modulate_2(h_ctx, m_ctx[0], m_ctx[1])
        if is_even:
            e = layer // 2
            y_lat, y_ctx = _attn_pool_mixer(u_lat, u_ctx, cos, sin, w_mix_in[e], q_norm_g[e], k_norm_g[e],
                                            w_pool_grp[e], pool_scale[e], w_mix_out[e], ctx_out)
        else:
            o = layer // 2
            y_lat = _short_conv_mixer(u_lat, w_conv_in[o], conv_w[o], w_conv_out[o])
            y_ctx = _short_conv_mixer(u_ctx, w_conv_in[o], conv_w[o], w_conv_out[o]) if ctx_out else None
        h_lat = _post_norm_2(h_lat, m_lat[2] * y_lat, ln_mix_g[layer], ln_mix_b[layer])
        f_lat = _expert_choice_ffn(_modulate_2(h_lat, m_lat[3], m_lat[4]), w_router[layer],
                                   w_exp_gate[layer], w_exp_up[layer], w_exp_down[layer])
        h_lat = _post_norm_2(h_lat, m_lat[5] * f_lat, ln_ffn_g[layer], ln_ffn_b[layer])
        if ctx_out:
            h_ctx = _post_norm_2(h_ctx, m_ctx[2] * y_ctx, ln_mix_g[layer], ln_mix_b[layer])
            f_ctx = _expert_choice_ffn(_modulate_2(h_ctx, m_ctx[3], m_ctx[4]), w_router[layer],
                                       w_exp_gate[layer], w_exp_up[layer], w_exp_down[layer])
            h_ctx = _post_norm_2(h_ctx, m_ctx[5] * f_ctx, ln_ffn_g[layer], ln_ffn_b[layer])
    return h_lat


def setup_inputs(seed=0):
    out = dict(first_inputs(seed))
    for name, value in second_inputs(seed + 1).items():
        if name != "x":
            out[name + "_2"] = value
    return out


def reference(
    x, c, w_ada, b_ada, ln_gain, ln_bias, ffn1_w_gate, ffn1_w_up, ffn1_w_down, w_in, w_out,
    ffn2_w_gate, ffn2_w_up, ffn2_w_down, c_2, ctx_2, c_ctx_2, w_mod_2, b_mod_2, ln_mix_g_2,
    ln_mix_b_2, ln_ffn_g_2, ln_ffn_b_2, w_mix_in_2, q_norm_g_2, k_norm_g_2, w_pool_grp_2,
    pool_scale_2, w_mix_out_2, w_conv_in_2, conv_w_2, w_conv_out_2, w_router_2, w_exp_gate_2,
    w_exp_up_2, w_exp_down_2,
):
    x = first_block(
        x, c, w_ada, b_ada, ln_gain, ln_bias, ffn1_w_gate, ffn1_w_up, ffn1_w_down, w_in, w_out,
        ffn2_w_gate, ffn2_w_up, ffn2_w_down,
    )
    return second_block(
        x, c_2, ctx_2, c_ctx_2, w_mod_2, b_mod_2, ln_mix_g_2, ln_mix_b_2, ln_ffn_g_2,
        ln_ffn_b_2, w_mix_in_2, q_norm_g_2, k_norm_g_2, w_pool_grp_2, pool_scale_2, w_mix_out_2,
        w_conv_in_2, conv_w_2, w_conv_out_2, w_router_2, w_exp_gate_2, w_exp_up_2, w_exp_down_2,
    )


_drawn_inputs = setup_inputs


def setup_inputs(seed=0):
    import zlib

    import numpy as np

    out = dict(_drawn_inputs(seed))
    spreads = {}
    factors = {'b_ada': 5.326,
     'ctx_2': 8.0,
     'c_ctx_2': 5.193,
     'b_mod_2': 8.0,
     'q_norm_g_2': 8.0,
     'k_norm_g_2': 8.0,
     'pool_scale_2': 8.0}
    for name, (base, spread) in spreads.items():
        noise = np.random.default_rng([zlib.crc32(name.encode()), seed]).standard_normal(out[name].shape)
        drawn = base * np.exp(spread * noise) if base else spread * noise
        out[name] = __import__('jax').numpy.asarray(drawn.astype(out[name].dtype))
    for name, factor in factors.items():
        out[name] = (out[name] * factor).astype(out[name].dtype)
    return out
```

```python
from contextlib import ExitStack

import numpy as np

import concourse.bass as bass
from concourse import mybir

F32 = mybir.dt.float32
ALU = mybir.AluOpType
ACT = mybir.ActivationFunctionType
AX_X = mybir.AxisListType.X

P = 128
S = 256
TT = S // P
D = 1024
KC = D // P
FF = 2816
TILES = FF // P
STEP = 2 * P
PAIRS = (TILES - 2) // 4
LAYERS = 2
HD = 64
RDV = 128
NH = 4
IN_W = 3072
MIX2_W = 1280
QH = 8
EXPERTS = 16
CAP = 2 * S // EXPERTS
NEG = -1.0e30
ALPHA = (2.0 * LAYERS) ** 0.25
LN_EPS, GN_EPS, NORM_EPS = 1e-5, 1e-6, 1e-6

RQ, RK, RV, RG, DQ, DK, DV, SQ, SK, SV = 0, 256, 512, 1024, 1536, 1792, 2048, 2304, 2560, 2816
RET, DIL, STB = 0, 1, 2
QCOL, KCOL, VCOL, VW = (RQ, DQ, SQ), (RK, DK, SK), (RV, DV, SV), (RDV, HD, HD)

MOD2 = 9 * LAYERS
CTX_ROW = MOD2 + 6 * LAYERS
JOBS = CTX_ROW + 2
FIRST_JOBS = 2
JOBS_1, JOBS_2 = 2 * PAIRS, PAIRS
JOBS_LAYER = JOBS_1 + JOBS_2
assert FIRST_JOBS + LAYERS * JOBS_LAYER == JOBS

MIX_SLOT0, MIX_SLOTS = 6, 6
MIX_IN_USES = IN_W * D // (P * 2048)
MIX_USES = MIX_IN_USES + D * D // (P * 2048)
PER_LAYER = [sum(1 for u in range(MIX_USES) if u % MIX_SLOTS == s) for s in range(MIX_SLOTS)]
SLOTS = 12

ATT = [(DIL, 0), (STB, 0), (DIL, 1), (STB, 1), (RET, 0), (RET, 1)]


class Steps:

    def __init__(self, sem, names):
        self.s, self.names, self.next = sem, list(names), 0

    def at(self, name, inst=0):
        return inst * len(self.names) + self.names.index(name) + 1

    def sig(self, name):
        assert self.names[self.next] == name, (self.names[self.next], name)
        self.next = (self.next + 1) % len(self.names)
        return self.s


def stack_constants():
    i = np.arange(P, dtype=np.float64)
    t = np.arange(S, dtype=np.float32)
    out = {}
    out["ident"] = np.eye(P, dtype=np.float32)
    out["ones"] = np.ones((P, P), np.float32)
    out["later"] = (i[:, None] > i[None, :]).astype(np.float32)
    out["strict"] = (i[:, None] < i[None, :]).astype(np.float32)
    lg = np.log1p(-np.exp2(-5.0 - np.arange(NH)))
    ret = np.zeros((P, NH, S))
    for h in range(NH):
        dist = np.arange(S)[None, :] - i[:, None]
        ret[:, h] = np.where(dist >= 0, np.exp(lg[h] * np.maximum(dist, 0)), 0.0) * HD ** -0.5
    out["decay"] = ret.astype(np.float32)
    dist = i[:, None] + P - np.arange(S)[None, :]
    cnt = np.zeros((P, S))
    for w, dl in zip((128, 512, 2048), (1, 4, 16)):
        cnt += (dist >= 0) & (dist % dl == 0) & (dist <= w)
    out["windows"] = cnt.astype(np.float32)
    out["closed"] = np.where(cnt > 0, 0.0, NEG).astype(np.float32)

    def rope(freq):
        ang = (t[:, None] * freq[None, :].astype(np.float32)).astype(np.float32).astype(np.float64)
        return np.cos(ang), np.sin(ang)

    def tiles(a):
        return a.reshape(TT, P, -1).transpose(1, 0, 2).astype(np.float32)
    f32 = np.float32
    rows = []
    for freq in (1.0 / f32(10000.0) ** np.linspace(0.0, 1.0, 32, dtype=f32),
                 1.0 / f32(10000.0) ** (np.arange(0, HD, 2, dtype=f32) / f32(HD))):
        c, s = rope(freq)
        rows += [tiles(c), tiles(s)]
    out["rope1"] = np.stack(rows, 1)
    f = f32(10000.0) ** (-np.arange(0, 32, 2, dtype=f32) / f32(32))
    row, col = np.repeat(np.arange(S // 64), 64).astype(f32), np.tile(np.arange(64), S // 64).astype(f32)
    ang = np.concatenate([(row[:, None] * f), (col[:, None] * f)], 1).astype(f32).astype(np.float64)
    out["rope2"] = np.stack([tiles(np.cos(ang)), tiles(np.sin(ang))], 1)
    out["slot_no"] = np.tile((np.arange(P) % CAP + 1).astype(np.float32), (P, 1))
    pool = np.zeros((4, S, S))
    for g, w in enumerate((2, 4, 8, 16)):
        for q in range(S):
            lo, hi = max(q - w // 2, 0), min(q + w // 2, S)
            pool[g, lo:hi, q] += 1.0 / (hi - lo)
            pool[g, q, q] -= 1.0
    out["pool"] = pool.reshape(4, TT, P, S).transpose(2, 0, 1, 3).astype(np.float32)
    return out



CONSTS = ("ident", "ones", "later", "strict", "decay", "windows", "closed", "rope1")
CONSTS2 = ("pool", "w_grp", "rope2", "qk_gain", "p_scale", "w_router", "conv_w", "slot_no")


def build(nc, A, out):
    with ExitStack() as ctx:
        def sb(name, shape):
            return ctx.enter_context(nc.sbuf_tensor(name, shape, F32))

        def sem(name):
            return ctx.enter_context(nc.semaphore(name))

        def steps(name, names):
            return Steps(sem(name), names)

        ds = bass.ds
        ctx.enter_context(nc.allow_non_contiguous_dma(reason="modulation rows are read as columns"))
        mod_rows = nc.dram_tensor("mod_rows", [JOBS, D], F32, kind="Internal").ap()

        W = sb("W", [P, SLOTS, 2048])
        W_mod = sb("W_mod", [P, 2, 2048])
        x_tok = sb("x_tok", [P, TT, D])
        uT = sb("uT", [P, KC, S])
        tmp = sb("tmp", [P, TT, D])
        y_tok = tmp
        gate_row = sb("gate_row", [P, D])
        gain_row = sb("gain_row", [P, D])
        mod_acc = sb("mod_acc", [P, D])
        mod_bias = sb("mod_bias", [P, D])
        cond = sb("cond", [P, JOBS, KC])
        cond_now = sb("cond_now", [P, KC])
        cvec = sb("cvec_sb", [P, 2, 3, KC])
        shift_c = sb("shift_c", [P, KC])
        scale_c = sb("scale_c", [P, KC])
        stats = sb("stats", [P, 8, 6])
        mv = sb("mv", [P, 8, 2])
        rstd = sb("rstd", [P, 8])
        neg_max = sb("neg_max", [P, 2, 4])
        den = sb("den", [P, 16])
        key_max = sb("key_max", [P, 16])
        K = {n: sb("k_" + n, list(A[n].shape)) for n in CONSTS}
        qm = sb("qm", [P, 12, S])
        SCR = 7680
        scr = sb("scr", [P, SCR])
        psum = ctx.enter_context(nc.psum_tensor("psum", [P, 8, 512], F32))

        def part(of, at, *shape):
            n = int(np.prod(shape))
            v = of[:, at:at + n]
            names = "abc"[:len(shape)]
            if len(shape) > 1:
                v = v.rearrange(f"p ({' '.join(names)}) -> p {' '.join(names)}", **dict(zip(names[:-1], shape)))
            return v

        def carve(at, *shape):
            assert at + int(np.prod(shape)) <= SCR, (at, shape)
            return part(scr, at, *shape)

        silu_g = carve(0, 2, S)
        hT = carve(512, 2, S)
        mod_out = carve(1024, 512)
        proj = carve(0, TT, IN_W)
        kT = carve(6144, 6, S)
        att = [part(mod_acc, 0, 2, 3 * P), y_tok[:, :, 0:3 * P]]
        dil_pT = proj[:, :, 0:3 * P]
        stb_z = proj[:, :, DQ:DQ + 3 * P]
        stb_l = proj[:, :, SQ:SQ + 3 * P]
        rope_a, rope_b = tmp[:, 0, 0:512], tmp[:, 1, 0:512]
        proj2 = carve(0, TT, MIX2_W)
        ctx_kv = carve(2560, TT, 256)
        kT2 = carve(3072, 512)
        prob = carve(3584, 2, 512)
        probT = carve(4608, 2, 512)
        ctx_uT = carve(5632, KC, S)
        squares = carve(5632, TT, 12 * HD)
        pooledT = part(mod_acc, 0, 4, S)
        ctx_tok = tmp
        wm0, wm1 = W_mod[:, 0, :], W_mod[:, 1, :]
        pool_c = part(wm0, 0, 4, TT, S)
        w_grp = part(wm1, 0, 4, P)
        rope2 = part(wm1, 512, 2, TT, 32)
        qk_gain = part(wm1, 640, 2, HD)
        p_scale = wm1[:, 768:772]
        routeT = part(wm1, 800, 2, 32)
        slot_no = wm1[:, 880:1008]
        route = part(wm1, 1024, 4, S)
        w_router = part(mod_bias, 0, LAYERS, KC * EXPERTS)
        conv_w = part(mod_bias, 256, KC, 3)
        top8 = mod_bias[:, 300:308]
        conv_s = carve(0, 2, S + 2)
        conv_b = carve(600, 2, S)
        conv_c = carve(1200, 2, S)
        conv_z = carve(1800, 2, S)
        conv_yT = carve(3000, KC, S)
        xeT = carve(0, KC, EXPERTS * CAP)
        xe_now = carve(4096, KC, CAP)
        e_silu = carve(4352, S)
        e_h = carve(4608, S)
        e_hT = carve(4864, 2, P)
        R = carve(5120, D)
        G_now = carve(6144, TT, P)
        GT = carve(6400, S)
        sel = carve(6656, TT, EXPERTS * CAP)

        s_const = sem("constants_loaded")
        s_const2 = sem("constants2_loaded")
        s_x = sem("x_loaded")
        landed = [sem(f"landed{s}") for s in range(SLOTS)]
        mod_landed = [sem(f"mod_landed{s}") for s in range(2)]
        mod_freed = [sem(f"mod_freed{s}") for s in range(2)]
        bias_landed = sem("mod_bias_landed")
        zeroed = sem("zeroed")
        cond_sig = sem("cond_sigmoid")
        cond_read = sem("mod_started")
        mod_ready = sem("mod_acc_ready")
        mod_summed = sem("mod_summed")
        mod_taken = sem("mod_taken")
        mod_stored = sem("mod_stored")
        pe_gu = sem("pe_gate_up")
        act_silu = sem("act_silu")
        dve_h = sem("dve_hidden")
        pe_down = sem("pe_down")
        cols_landed = sem("shift_scale_landed")
        cols_ready = sem("scale_plus_one")
        rows_landed = sem("gate_gain_landed")
        gated = sem("gate_applied")
        lnb_landed = sem("ln_bias_landed")
        pn_var = sem("norm_variance")
        pn_sqrt = sem("norm_sqrt")
        pn_x = sem("x_tok_tiles")
        tr_pe = sem("turned_banks")
        tr_act = sem("uT_half_act")
        tr_dve = sem("uT_half_dve")
        s_out = sem("out_stored")

        m_pe = steps("mixer_pe", [f"proj{n}" for n in range(12)] + [f"qk{g}" for g in range(6)] + ["A0", "A1"]
                     + sum([([f"B{b}"] if b < 4 else []) + [f"C{b}"] + ([f"A{b + 2}"] if b < 4 else [])
                            for b in range(6)], []) + ["out"])
        m_act = steps("mixer_act", [f"ev{n}" for n in range(12)] + ["silu_g", "qk0", "qk2", "qk4", "exp0", "ln1",
                                    "PT0", "exp2", "a1", "PT2", "ln3", "a3", "gn_sqrt"])
        m_dve = steps("mixer_dve", ["rot0", "rot1", "qk1", "qk3", "qk5", "max0", "na1", "p0", "lk1", "max2", "y0",
                                    "s1", "am1", "p2", "na3", "y1", "lk3", "y2", "s3", "r4", "am3", "r5", "y3",
                                    "gn_var", "y"])
        P2 = [f"c{t}" for t in range(TT)] + [f"p{t}{g}" for t in range(TT) for g in range(3)]
        m2_pe = steps("mix2_pe", P2 + ["pool0", "pool1", "grp0", "grp1", "kT", "q"] + ["S0", "S1"]
                      + sum([[f"T{n}", f"V{n}"] + ([f"S{n + 2}"] if n < 14 else []) for n in range(16)], [])
                      + ["yT0", "yT1", "out"])
        m2_act = steps("mix2_act", P2 + ["grp0", "grp1", "rms", "kT", "q"]
                       + sum([[f"e{n}", f"PT{n}"] for n in range(16)], []) + ["yT0"])
        m2_dve = steps("mix2_dve", ["pool0", "pool1", "sq", "rope", "q"] + [f"max{n}" for n in range(16)]
                       + ["y", "yT1"])
        cv_pe = steps("conv_pe", [f"f{fb}" for fb in range(KC)] + ["out"])
        cv_act = steps("conv_act", [f"f{fb}" for fb in range(KC)])
        cv_dve = steps("conv_dve", [f"f{fb}" for fb in range(KC)])
        r_pe = steps("router_pe", ["logits", "affT", "slotT"] + [f"g{k}" for k in range(KC)])
        r_act = steps("router_act", ["exp"] + [f"g{k}" for k in (0, 2, 4, 6)])
        r_dve = steps("router_dve", ["max", "aff", "slot", "sel"] + [f"g{k}" for k in (1, 3, 5, 7)])
        e_pe = steps("expert_pe", [f"k{k}" for k in range(KC)] + ["gT", "hT"] + [f"d{q}" for q in range(4)] + ["out"])
        e_act = steps("expert_act", ["silu", "hT", "R"])
        e_dve = steps("expert_dve", ["xG", "h", "gT", "R"])

        FFN_TILES = 2 * LAYERS * TILES
        MIXIN_S, MIXOUT_S = (6, 7, 8, 9, 10), (11, 0, 1, 2)

        fills = [2 * (2 * PAIRS + 1)] * MIX_SLOT0 + [LAYERS * c for c in PER_LAYER]
        before = {}
        for phase, slots_, units in (("in", MIXIN_S, 1), ("out", MIXOUT_S, 1), ("moe0", range(SLOTS), 2 * EXPERTS),
                                     ("cin", range(SLOTS), 1), ("cout", range(4), 1),
                                     ("moe1", range(SLOTS), 2 * EXPERTS)):
            for s in slots_:
                before[phase, s] = fills[s]
                fills[s] += units

        def slot_landed(phase, s, e=0):
            units = 2 * e + 2 if phase.startswith("moe") else 1
            return 16 * before[phase, s] + 16 * units

        block = ctx.enter_context(nc.Block())

        @block.sync
        def _(sp):
            sp.dma_start(x_tok[:, :, :], A["x"].rearrange("(t p) d -> p t d", p=P)).then_inc(s_x, 16)
            sp.wait_ge(zeroed, 3)

            def mod_chunk(job, c, first=None):
                if first is None or 2 * first + c // 2 > 0:
                    sp.wait_ge(mod_freed[c % 2], 2 * job + c // 2)
                if c == 0:
                    if first != 0:
                        sp.wait_ge(cond_read, job)
                    sp.dma_start(mod_bias[0:1, :], A["mod_b"][ds(job, 1), :]).then_inc(bias_landed, 16)
                src = A["mod_w"][ds(job, 1), 256 * c:256 * c + 256, :]
                sp.dma_start(part(W_mod[:, c % 2, :], 0, 2, D), src.rearrange("a (k p) n -> p (a k) n", p=P)
                             ).then_inc(mod_landed[c % 2], 16)

            for job in range(FIRST_JOBS):
                for c in range(4):
                    mod_chunk(job, c, job)

            def step_weights(l, k, parity, j, used):
                names = ("ffn1_w_gate", "ffn1_w_up", "ffn1_w_down") if k == 0 else ("ffn2_w_gate", "ffn2_w_up", "ffn2_w_down")
                b = 3 * ((parity + k) % 2)
                sp.wait_ge(pe_gu, used)
                for n in range(2):
                    src = A[names[n]][ds(l, 1), :, ds(j * STEP, STEP)]
                    sp.dma_start(part(W[:, b + n, :], 0, KC, STEP), src.rearrange("a (k p) n -> p (a k) n", p=P)
                                 ).then_inc(landed[b + n], 16)
                sp.wait_ge(pe_down, used)
                src = A[names[2]][ds(l, 1), ds(j * STEP, STEP), :]
                sp.dma_start(part(W[:, b + 2, :], 0, 2, D), src.rearrange("a (k p) n -> p (a k) n", p=P)
                             ).then_inc(landed[b + 2], 16)

            def ffn_stream(l, k):
                base = 1 + l * (2 * TILES) + k * TILES
                step_weights(l, k, 0, 0, base)
                with sp.Fori(0, PAIRS) as i:
                    for r in range(2):
                        step_weights(l, k, r + 1, i * 2 + (r + 1), base + i * 4 + 2 * r)
                        if k == 0:
                            for c in range(4):
                                mod_chunk(l * JOBS_LAYER + i * 2 + (FIRST_JOBS + r), c)
                        else:
                            for c in (2 * r, 2 * r + 1):
                                mod_chunk(l * JOBS_LAYER + i + (FIRST_JOBS + JOBS_1), c)

            with sp.Fori(0, LAYERS) as l:
                ffn_stream(l, 0)
                for u in range(MIX_USES):
                    s = MIX_SLOT0 + u % MIX_SLOTS
                    last = u - MIX_SLOTS
                    if last < 0:
                        sp.wait_ge(pn_x, l * 6 + 2)
                    else:
                        sp.wait_ge(m_pe.s, m_pe.at(f"proj{2 * (last // 2) + 1}", l))
                    if u < MIX_IN_USES:
                        g, half = u // 2, u % 2
                        src = A["w_in"][ds(l, 1), 512 * half:512 * half + 512, 512 * g:512 * g + 512]
                        dst = part(W[:, s, :], 0, 4, 512)
                    else:
                        r0 = 256 * (u - MIX_IN_USES)
                        src = A["w_out"][ds(l, 1), r0:r0 + 256, :]
                        dst = part(W[:, s, :], 0, 2, D)
                    sp.dma_start(dst, src.rearrange("a (k p) n -> p (a k) n", p=P)).then_inc(landed[s], 16)
                ffn_stream(l, 1)

            sp.wait_ge(m_pe.s, m_pe.at("out", LAYERS - 1))
            for g, s in enumerate(MIXIN_S):
                sp.dma_start(part(W[:, s, :], 0, KC, 256),
                             A["w_mix_in"][:, 256 * g:256 * g + 256].rearrange("(k p) n -> p k n", p=P)
                             ).then_inc(landed[s], 16)

            def rows_of(w, s, g):
                sp.dma_start(part(W[:, s, :], 0, 2, D), w[256 * g:256 * g + 256, :].rearrange("(k p) n -> p k n", p=P)
                             ).then_inc(landed[s], 16)

            rows_of(A["w_mix_out"], MIXOUT_S[0], 0)
            sp.wait_ge(pe_gu, 1 + FFN_TILES)
            sp.wait_ge(pe_down, 1 + FFN_TILES)
            for g in range(1, 4):
                rows_of(A["w_mix_out"], MIXOUT_S[g], g)

            def expert_slot(layer, e, s):
                if s < KC:
                    for n, w in enumerate((A["w_exp_gate"], A["w_exp_up"])):
                        sp.dma_start(W[:, s, D * n:D * n + D], w[layer, ds(e, 1), P * s:P * s + P, :]
                                     .rearrange("a p n -> p (a n)")).then_inc(landed[s], 16)
                else:
                    r0 = 256 * (s - KC)
                    sp.dma_start(part(W[:, s, :], 0, 2, D), A["w_exp_down"][layer, ds(e, 1), r0:r0 + 256, :]
                                 .rearrange("a (k p) n -> p (a k) n", p=P)).then_inc(landed[s], 32)

            def slot_use(s):
                return f"k{s}" if s < KC else f"d{s - KC}"

            def expert_stream(layer, first_wait):
                for s in first_wait:
                    sem_, n = first_wait[s]
                    sp.wait_ge(sem_, n)
                    expert_slot(layer, 0, s)
                with sp.Fori(1, EXPERTS) as e:
                    for s in range(SLOTS):
                        sp.wait_ge(e_pe.s, e_pe.at(slot_use(s), e + (EXPERTS * layer - 1)))
                        expert_slot(layer, e, s)

            free = {s: (pe_down, 1 + FFN_TILES) for s in (3, 4, 5)}
            free |= {s: (m2_pe.s, m2_pe.at("p12")) for s in MIXIN_S}
            free |= {s: (m2_pe.s, m2_pe.at("out")) for s in MIXOUT_S}
            expert_stream(0, dict(sorted(free.items(), key=lambda f: f[1][1] if f[1][0] is m2_pe.s else -1)))
            for u in range(12):
                sp.wait_ge(e_pe.s, e_pe.at(slot_use(u), EXPERTS - 1))
                c0 = D * (u % 3) + 256 * (u // 3)
                sp.dma_start(part(W[:, u, :], 0, KC, 256), A["w_conv_in"][:, c0:c0 + 256]
                             .rearrange("(k p) n -> p k n", p=P)).then_inc(landed[u], 16)
            for s in range(4):
                sp.wait_ge(cv_pe.s, cv_pe.at(f"f{2 * (s // 3) + 1}"))
                rows_of(A["w_conv_out"], s, s)
            free = {s: (cv_pe.s, cv_pe.at(f"f{2 * (s // 3) + 1}")) for s in range(4, SLOTS)}
            free |= {s: (cv_pe.s, cv_pe.at("out")) for s in range(4)}
            expert_stream(1, free)
            sp.wait_ge(pn_x, 2 + 2 * 10)
            sp.dma_start(out.rearrange("(t p) d -> p t d", p=P), x_tok[:, :, :]).then_inc(s_out, 16)
            sp.wait_ge(s_out, 16)

        @block.gpsimd
        def _(pool):
            pool.dma_start(cvec[:, 0, :, :], A["cvec"]).then_inc(s_const, 16)
            for name in CONSTS:
                pool.dma_start(K[name][:], A[name]).then_inc(s_const, 16)
            pool.memset(mod_bias[:, :], 0.0).then_inc(zeroed, 1)
            pool.memset(qm[:, 0:6, :], 0.0).then_inc(zeroed, 1)
            pool.memset(qm[:, 6:12, :], 0.0).then_inc(zeroed, 1)

            def columns(row, need=None):
                if need is not None:
                    pool.wait_ge(mod_stored, need)
                    pool.wait_ge(zeroed, 3)
                for n, dst in enumerate((shift_c, scale_c)):
                    pool.dma_start(dst[:, :], mod_rows[ds(row + n, 1), :].rearrange("a (k p) -> p (a k)", p=P)
                                   ).then_inc(cols_landed, 16)

            def rows(p, row, need=None):
                if need is not None:
                    pool.wait_ge(mod_stored, need)
                pool.wait_ge(pn_x, p * 2 + 2)
                pool.wait_ge(zeroed, 3)
                pool.dma_start(gate_row[:, :], mod_rows[ds(row, 1), :].to_broadcast([P, D])).then_inc(rows_landed, 16)
                pool.dma_start(gain_row[:, :], A["ln_g"][ds(p, 1), :].to_broadcast([P, D])).then_inc(rows_landed, 16)

            with pool.Fori(0, LAYERS) as l:
                for k in range(3):
                    turned = l * 4 + (1 + (k if k < 2 else 3))
                    pool.wait_ge(tr_act, turned)
                    pool.wait_ge(tr_dve, turned)
                    columns(l * 9 + 3 * k, l * (9 * 16) + 16 * (3 * k + 2))
                    rows(l * 3 + k, l * 9 + (3 * k + 2), l * (9 * 16) + 16 * (3 * k + 3))
            for c, (p, turned) in enumerate(((6, 9), (7, 11), (8, 12), (9, 13))):
                row = MOD2 + 3 * c
                pool.wait_ge(tr_act, turned)
                pool.wait_ge(tr_dve, turned)
                if c == 2:
                    pool.wait_ge(r_act.s, r_act.at("g6"))
                    pool.wait_ge(r_dve.s, r_dve.at("g7"))
                columns(row, 16 * JOBS if c == 0 else None)
                rows(p, row + 2)
                if c == 0:
                    for n in CONSTS2:
                        dst = {"pool": pool_c, "w_grp": w_grp, "rope2": rope2, "qk_gain": qk_gain, "p_scale": p_scale,
                               "w_router": w_router, "conv_w": conv_w, "slot_no": slot_no}[n]
                        pool.dma_start(dst, A[n]).then_inc(s_const2, 16)
                    pool.dma_start(ctx_tok[:, :, :], A["ctx"].rearrange("(t p) d -> p t d", p=P)).then_inc(s_const2, 16)
                    pool.wait_ge(tr_act, 10)
                    pool.wait_ge(tr_dve, 10)
                    columns(CTX_ROW)

        @block.tensor
        def _(pe):
            pe.wait_ge(s_const, 16 * (len(CONSTS) + 1))
            ident = K["ident"]

            def mod_sum(job, first=False):
                pe.wait_ge(mod_ready, job + 1)
                if not first:
                    pe.wait_ge(mod_taken, job * 2)
                for h in range(2):
                    ins = pe.matmul(psum[32 * h:32 * h + 1, 6, :], K["ones"][:, 0:1], mod_acc[:, 512 * h:512 * h + 512],
                                    start=True, stop=True)
                ins.then_inc(mod_summed, 1)

            def turn(src, ready):
                for b in range(4):
                    for q in range(2):
                        for t in range(TT):
                            if b == 0 and q == 0:
                                pe.wait_ge(*ready(t))
                            c = P * (2 * b + q)
                            ins = pe.transpose(psum[:, 4 + b, S * q + P * t:S * q + P * t + P], src[:, t, c:c + P], ident[:, :])
                    ins.then_inc(tr_pe, 1)

            def turned(inst):
                pe.wait_ge(tr_act, inst + 2)
                pe.wait_ge(tr_dve, inst + 2)

            def ffn(l, k):
                f0 = 1 + l * (2 * TILES) + k * TILES
                fill0 = [l * (2 * PAIRS + 1) + (0, PAIRS + 1 - q)[k] for q in range(2)]

                def slots_of(t, i=0):
                    q = (t // 2 + k) % 2
                    return 3 * q, (fill0[q] + i + (t // 4 + 1)) * 16

                def gate_up(t, i=0):
                    b, n = slots_of(t, i)
                    if t % 2 == 0:
                        pe.wait_ge(landed[b], n)
                        pe.wait_ge(landed[b + 1], n)
                    if t >= 2:
                        pe.wait_ge(dve_h, f0 + i * 4 + (t - 1))
                    for g in range(2):
                        w = part(W[:, b + g, :], 0, KC, STEP)
                        for kc in range(KC):
                            ins = pe.matmul(psum[:, 4 + t % 2, S * g:S * g + S], w[:, kc, P * (t % 2):P * (t % 2) + P],
                                            uT[:, kc, :], start=(kc == 0), stop=(kc == KC - 1))
                    ins.then_inc(pe_gu, 1)

                def down(t, i=0):
                    b, n = slots_of(t, i)
                    if t % 2 == 0:
                        pe.wait_ge(landed[b + 2], n)
                    pe.wait_ge(dve_h, f0 + i * 4 + (t + 1))
                    w = part(W[:, b + 2, :], 0, 2, D)
                    for tt in range(TT):
                        for h in range(2):
                            ins = pe.matmul(psum[:, 2 * tt + h, :], hT[:, t % 2, P * tt:P * tt + P],
                                            w[:, t % 2, 512 * h:512 * h + 512], start=(t == 0), stop=(t == TILES - 1),
                                            skip_group_check=True)
                    ins.then_inc(pe_down, 1)

                gate_up(0)
                gate_up(1)
                down(0)
                with pe.Fori(0, PAIRS) as i:
                    for t in range(1, 5):
                        gate_up(t + 1, i)
                        if k == 0 and t % 2 == 0:
                            mod_sum(l * JOBS_LAYER + i * 2 + (FIRST_JOBS + t // 2 - 1))
                        if k == 1 and t == 4:
                            mod_sum(l * JOBS_LAYER + i + (FIRST_JOBS + JOBS_1))
                        down(t, i)
                down(TILES - 1)
                pe.wait_ge(mod_taken, (l * JOBS_LAYER + (FIRST_JOBS + JOBS_1 + JOBS_2 * k)) * 2)

            def times_rows(src, slots):
                for u in range(4):
                    w = part(W[:, slots(u), :], 0, 2, D)
                    for kk in range(2):
                        kc = 2 * u + kk
                        for tt in range(TT):
                            for h in range(2):
                                ins = pe.matmul(psum[:, 2 * tt + h, :], src[:, kc, P * tt:P * tt + P],
                                                w[:, kk, 512 * h:512 * h + 512], start=(kc == 0), stop=(kc == KC - 1),
                                                skip_group_check=True)
                return ins

            def mixer(l):
                def slot(u):
                    s = u % MIX_SLOTS
                    pe.wait_ge(landed[MIX_SLOT0 + s], (l * PER_LAYER[s] + (u // MIX_SLOTS + 1)) * 16)
                    return MIX_SLOT0 + s

                for g in range(6):
                    for t in range(TT):
                        n = 2 * g + t
                        if n >= 4:
                            pe.wait_ge(m_act.s, m_act.at(f"ev{n - 4}", l))
                        for kc in range(KC):
                            u = 2 * g + kc // 4
                            s = slot(u) if kc % 4 == 0 else MIX_SLOT0 + u % MIX_SLOTS
                            ins = pe.matmul(psum[:, 4 + n % 4, :], uT[:, kc, P * t:P * t + P],
                                            part(W[:, s, :], 0, 4, 512)[:, kc % 4, :], start=(kc == 0), stop=(kc == KC - 1))
                        ins.then_inc(m_pe.sig(f"proj{n}"), 1)
                for g in range(6):
                    kind, hb = g // 2, g % 2
                    if g < 4:
                        pe.wait_ge(m_act.s, m_act.at(f"ev{8 + g}", l))
                    if g == 0:
                        pe.wait_ge(m_dve.s, m_dve.at("rot0", l))
                    if g == 2:
                        pe.wait_ge(m_dve.s, m_dve.at("rot1", l))
                    if g == 4:
                        pe.wait_ge(m_act.s, m_act.at("qk0", l))
                        pe.wait_ge(m_act.s, m_act.at("ev11", l))
                    if g == 5:
                        pe.wait_ge(m_dve.s, m_dve.at("qk1", l))
                    for n, col in enumerate((QCOL[kind], KCOL[kind])):
                        for t in range(TT):
                            ins = pe.transpose(psum[:, 4 + g % 4, S * n + P * t:S * n + P * t + P],
                                               proj[:, t, col + P * hb:col + P * hb + P], ident[:, :])
                    ins.then_inc(m_pe.sig(f"qk{g}"), 1)

                def scores(b):
                    kind, hb = ATT[b]
                    for hh in range(2):
                        q, k_ = qm[:, NH * kind + 2 * hb + hh, :], kT[:, 2 * kind + hb, :]
                        bk = psum[:, 4 + 2 * (b % 2) + hh, :]
                        if kind == DIL:
                            pe.matmul(bk[:, 0:P], q[:, 0:P], k_[:, 0:P], start=True, stop=True)
                            ins = pe.matmul(bk[:, P:3 * P], q[:, P:S], k_[:, :], start=True, stop=True)
                        else:
                            pe.matmul(bk[:, 0:S], k_[:, 0:P], q[:, :], start=True, stop=True)
                            ins = pe.matmul(bk[:, S:3 * P], k_[:, P:S], q[:, P:S], start=True, stop=True)
                    ins.then_inc(m_pe.sig(f"A{b}"), 1)

                def second(b):
                    kind, hb = ATT[b]
                    bk = psum[:, 4 + 2 * (b % 2):6 + 2 * (b % 2), :]
                    if kind == DIL:
                        pe.wait_ge(m_dve.s, m_dve.at(f"p{b}", l))
                        for hh in range(2):
                            for c in range(3):
                                ins = pe.transpose(bk[:, hh, P * c:P * c + P], att[b % 2][:, hh, P * c:P * c + P], ident[:, :])
                    else:
                        pe.wait_ge(m_dve.s, m_dve.at(f"lk{b}", l))
                        for hh in range(2):
                            lk = stb_z[:, hh, :]
                            pe.matmul(bk[:, hh, 0:3 * P], K["later"][:, :], lk, start=True, stop=False, skip_group_check=True)
                            ins = pe.matmul(bk[:, hh, P:S], K["ones"][:, :], lk[:, S:3 * P], start=False, stop=True,
                                            skip_group_check=True)
                    ins.then_inc(m_pe.sig(f"B{b}"), 1)

                def values(b):
                    kind, hb = ATT[b]
                    if kind == DIL:
                        pe.wait_ge(m_act.s, m_act.at(f"PT{b}", l))
                    elif kind == STB:
                        pe.wait_ge(m_dve.s, m_dve.at(f"am{b}", l))
                    else:
                        pe.wait_ge(m_dve.s, m_dve.at(f"r{b}", l))
                    for hh in range(2):
                        h, w = 2 * hb + hh, VW[kind]
                        pT = dil_pT[:, hh, :] if kind == DIL else att[b % 2][:, hh, :]
                        v = proj[:, :, VCOL[kind] + w * h:VCOL[kind] + w * h + w]
                        if kind == RET:
                            o = [psum[:, t, w * h:w * h + w] for t in range(TT)]
                        else:
                            o = [psum[:, 1 + kind, S * t + w * h:S * t + w * h + w] for t in range(TT)]
                        pe.matmul(o[0], pT[:, 0:P], v[:, 0, :], start=True, stop=True)
                        pe.matmul(o[1], pT[:, P:S], v[:, 0, :], start=True, stop=False)
                        ins = pe.matmul(o[1], pT[:, S:3 * P], v[:, 1, :], start=False, stop=True)
                    ins.then_inc(m_pe.sig(f"C{b}"), 1)

                for g in (2, 4):
                    pe.wait_ge(m_act.s, m_act.at(f"qk{g}", l))
                pe.wait_ge(m_dve.s, m_dve.at("qk5", l))
                scores(0)
                scores(1)
                for b in range(6):
                    if b < 4:
                        second(b)
                    if b == 2:
                        pe.wait_ge(m_dve.s, m_dve.at("y0", l))
                    if b == 3:
                        pe.wait_ge(m_dve.s, m_dve.at("y1", l))
                    values(b)
                    if b < 4:
                        if ATT[b][0] == STB:
                            pe.wait_ge(m_dve.s, m_dve.at(f"s{b}", l))
                        scores(b + 2)
                turn(y_tok, lambda t: (m_dve.s, m_dve.at("y", l)))
                turned(l * 4 + 2)
                times_rows(uT, lambda u: slot(MIX_IN_USES + u)).then_inc(m_pe.sig("out"), 1)

            for job in range(FIRST_JOBS):
                mod_sum(job, job == 0)
            pe.wait_ge(mod_taken, 2 * FIRST_JOBS)
            with pe.Fori(0, LAYERS) as l:
                turn(x_tok, lambda t: (pn_x, l * 6 + (t + 1)))
                turned(l * 4)
                ffn(l, 0)
                turn(x_tok, lambda t: (pn_x, l * 6 + (t + 3)))
                turned(l * 4 + 1)
                mixer(l)
                turn(x_tok, lambda t: (pn_x, l * 6 + (t + 5)))
                turned(l * 4 + 3)
                ffn(l, 1)

            turn(x_tok, lambda t: (pn_x, 12 + t + 1))
            turned(8)
            turn(ctx_tok, lambda t: (s_const2, 16 * (len(CONSTS2) + 1)))
            turned(9)

            def in_slot(phase, s):
                pe.wait_ge(landed[s], slot_landed(phase, s))
                return s
            for t in range(TT):
                s = in_slot("in", MIXIN_S[2]) if t == 0 else MIXIN_S[2]
                for kc in range(KC):
                    ins = pe.matmul(psum[:, 6 + t, 0:256], ctx_uT[:, kc, P * t:P * t + P], part(W[:, s, :], 0, KC, 256)[:, kc, :],
                                    start=(kc == 0), stop=(kc == KC - 1))
                ins.then_inc(m2_pe.sig(f"c{t}"), 1)
            for t in range(TT):
                for b in range(3):
                    for g in (2 * b, 2 * b + 1)[:1 if b == 2 else 2]:
                        s = in_slot("in", MIXIN_S[g]) if t == 0 else MIXIN_S[g]
                        for kc in range(KC):
                            ins = pe.matmul(psum[:, 3 * t + b, 256 * (g % 2):256 * (g % 2) + 256], uT[:, kc, P * t:P * t + P],
                                            part(W[:, s, :], 0, KC, 256)[:, kc, :], start=(kc == 0), stop=(kc == KC - 1))
                    ins.then_inc(m2_pe.sig(f"p{t}{b}"), 1)
            pe.wait_ge(m2_act.s, m2_act.at("p12"))
            for i in range(2):
                for g in (2 * i, 2 * i + 1):
                    for t in range(TT):
                        ins = pe.matmul(psum[:, 2 + i, S * (g % 2):S * (g % 2) + S], proj2[:, t, 768 + P * g:768 + P * g + P],
                                        pool_c[:, g, t, :], start=(t == 0), stop=(t == TT - 1))
                ins.then_inc(m2_pe.sig(f"pool{i}"), 1)
            for i in range(2):
                pe.wait_ge(m2_dve.s, m2_dve.at(f"pool{i}"))
                for g in (2 * i, 2 * i + 1):
                    ins = pe.matmul(psum[:, 2 + i, S * (g % 2):S * (g % 2) + S], w_grp[:, g, :], pooledT[:, g, :],
                                    start=True, stop=True)
                ins.then_inc(m2_pe.sig(f"grp{i}"), 1)
            pe.wait_ge(m2_dve.s, m2_dve.at("rope"))
            for n, src in enumerate((ctx_kv[:, 0, 0:P], ctx_kv[:, 1, 0:P], proj2[:, 0, 512:640], proj2[:, 1, 512:640])):
                ins = pe.transpose(psum[:, 4, P * n:P * n + P], src, ident[:, :])
            ins.then_inc(m2_pe.sig("kT"), 1)
            for j in range(4):
                for t in range(TT):
                    c = S * (j % 2) + P * t
                    ins = pe.transpose(psum[:, 5 + j // 2, c:c + P], proj2[:, t, P * j:P * j + P], ident[:, :])
            ins.then_inc(m2_pe.sig("q"), 1)
            pe.wait_ge(m2_act.s, m2_act.at("q"))
            pe.wait_ge(m2_dve.s, m2_dve.at("q"))

            def qk2(n):
                h, t = n // 2, n % 2
                pe.matmul(psum[:, 4 + n % 2, :], qm[:, 2 * (h % 4) + h // 4, P * t:P * t + P], kT2[:, :],
                          start=True, stop=True).then_inc(m2_pe.sig(f"S{n}"), 1)
            qk2(0)
            qk2(1)
            for n in range(16):
                h, t = n // 2, n % 2
                pe.wait_ge(m2_act.s, m2_act.at(f"e{n}"))
                for c in range(4):
                    ins = pe.transpose(psum[:, 6 + n % 2, P * c:P * c + P], prob[:, n % 2, P * c:P * c + P], ident[:, :])
                ins.then_inc(m2_pe.sig(f"T{n}"), 1)
                pe.wait_ge(m2_act.s, m2_act.at(f"PT{n}"))
                kv = 128 + HD * (h // 4)
                for c, v in enumerate((ctx_kv[:, 0, kv:kv + HD], ctx_kv[:, 1, kv:kv + HD],
                                       proj2[:, 0, 512 + kv:512 + kv + HD], proj2[:, 1, 512 + kv:512 + kv + HD])):
                    ins = pe.matmul(psum[:, t, HD * h:HD * h + HD], probT[:, n % 2, P * c:P * c + P], v,
                                    start=(c == 0), stop=(c == 3))
                ins.then_inc(m2_pe.sig(f"V{n}"), 1)
                if n < 14:
                    qk2(n + 2)
            pe.wait_ge(m2_dve.s, m2_dve.at("y"))
            for b in range(2):
                for q in range(2):
                    for t in range(TT):
                        c = P * (2 * b + q)
                        ins = pe.transpose(psum[:, 4 + b, S * q + P * t:S * q + P * t + P], proj2[:, t, c:c + P], ident[:, :])
                ins.then_inc(m2_pe.sig(f"yT{b}"), 1)
            pe.wait_ge(m2_act.s, m2_act.at("yT0"))
            pe.wait_ge(m2_dve.s, m2_dve.at("yT1"))
            times_rows(uT, lambda u: in_slot("out", MIXOUT_S[u])).then_inc(m2_pe.sig("out"), 1)

            def experts(layer):
                for t in range(TT):
                    for kc in range(KC):
                        ins = pe.matmul(psum[:, 4, EXPERTS * t:EXPERTS * t + EXPERTS], uT[:, kc, P * t:P * t + P],
                                        part(w_router[:, layer, :], 0, KC, EXPERTS)[:, kc, :], start=(kc == 0), stop=(kc == KC - 1))
                ins.then_inc(r_pe.sig("logits"), 1)
                pe.wait_ge(r_dve.s, r_dve.at("aff", layer))
                for t in range(TT):
                    ins = pe.transpose(psum[0:EXPERTS, 5, P * t:P * t + P], routeT[:, t, EXPERTS:2 * EXPERTS], ident[:, :])
                ins.then_inc(r_pe.sig("affT"), 1)
                pe.wait_ge(r_dve.s, r_dve.at("slot", layer))
                for t in range(TT):
                    ins = pe.transpose(psum[:, 5, EXPERTS * t:EXPERTS * t + EXPERTS], route[0:EXPERTS, 3, P * t:P * t + P],
                                       ident[0:EXPERTS, 0:EXPERTS])
                ins.then_inc(r_pe.sig("slotT"), 1)
                pe.wait_ge(r_dve.s, r_dve.at("sel", layer))
                for kc in range(KC):
                    for t in range(TT):
                        ins = pe.matmul(psum[:, kc, :], x_tok[:, t, P * kc:P * kc + P], sel[:, t, :],
                                        start=(t == 0), stop=(t == TT - 1))
                    ins.then_inc(r_pe.sig(f"g{kc}"), 1)
                pe.wait_ge(r_act.s, r_act.at("g6", layer))
                pe.wait_ge(r_dve.s, r_dve.at("g7", layer))

                def expert(e, first):
                    E = e + EXPERTS * layer
                    pe.wait_ge(e_dve.s, e_dve.at("xG", E))
                    for kc in range(KC):
                        pe.wait_ge(landed[kc], e * 32 + slot_landed(f"moe{layer}", kc))
                        w = part(W[:, kc, :], 0, 2, 4, 256)
                        for q in range(4):
                            ins = pe.matmul(psum[32 * q:32 * q + 32, 4, :].rearrange("p (g n) -> p g n", g=2),
                                            xe_now[:, kc, :], w[:, :, q, :], start=(kc == 0), stop=(kc == KC - 1),
                                            skip_group_check=True)
                        ins.then_inc(e_pe.sig(f"k{kc}"), 1)
                    for t in range(TT):
                        ins = pe.transpose(psum[:, 7, P * t:P * t + P], G_now[:, t, :], ident[:, :])
                    ins.then_inc(e_pe.sig("gT"), 1)
                    pe.wait_ge(e_dve.s, e_dve.at("h", E))
                    for j in range(2):
                        ins = pe.transpose(psum[:, 5, P * j:P * j + P], e_h[:, P * j:P * j + P], ident[:, :])
                    ins.then_inc(e_pe.sig("hT"), 1)
                    pe.wait_ge(e_act.s, e_act.at("hT", E))
                    for c in range(KC):
                        s = KC + c // 2
                        if c % 2 == 0:
                            pe.wait_ge(landed[s], e * 32 + slot_landed(f"moe{layer}", s))
                        for q in range(4):
                            ins = pe.matmul(psum[32 * q:32 * q + 32, 6, 0:256], e_hT[:, c % 2, 32 * (c // 2):32 * (c // 2) + 32],
                                            part(W[:, s, :], 0, 2, D)[:, c % 2, 256 * q:256 * q + 256],
                                            start=(c == 0), stop=(c == KC - 1), skip_group_check=True)
                        if c % 2:
                            ins.then_inc(e_pe.sig(f"d{c // 2}"), 1)
                    pe.wait_ge(e_act.s, e_act.at("R", E))
                    pe.wait_ge(e_dve.s, e_dve.at("R", E))
                    for tt in range(TT):
                        for h in range(2):
                            ins = pe.matmul(psum[:, 2 * tt + h, :], GT[:, P * tt:P * tt + P], R[:, 512 * h:512 * h + 512],
                                            start=first, stop=True, skip_group_check=True)
                    ins.then_inc(e_pe.sig("out"), 1)

                expert(0, True)
                with pe.Fori(1, EXPERTS) as e:
                    expert(e, False)

            turn(x_tok, lambda t: (pn_x, 14 + t + 1))
            turned(10)
            experts(0)

            turn(x_tok, lambda t: (pn_x, 16 + t + 1))
            turned(11)
            for fb in range(KC):
                if fb >= 2:
                    pe.wait_ge(cv_dve.s, cv_dve.at(f"f{fb - 2}"))
                for n in range(3):
                    s = 3 * (fb // 2) + n
                    if fb % 2 == 0:
                        in_slot("cin", s)
                    o = psum[:, 4 + 2 * (fb % 2) + n // 2, S * (n % 2):S * (n % 2) + S]
                    for kc in range(KC):
                        ins = pe.matmul(o, part(W[:, s, :], 0, KC, 256)[:, kc, P * (fb % 2):P * (fb % 2) + P], uT[:, kc, :],
                                        start=(kc == 0), stop=(kc == KC - 1))
                ins.then_inc(cv_pe.sig(f"f{fb}"), 1)
            pe.wait_ge(cv_dve.s, cv_dve.at("f7"))
            times_rows(conv_yT, lambda u: in_slot("cout", u)).then_inc(cv_pe.sig("out"), 1)
            turn(x_tok, lambda t: (pn_x, 18 + t + 1))
            turned(12)
            experts(1)

        @block.scalar
        def _(act):
            copy = ACT.Identity

            def mod_row(job, first=False):
                act.wait_ge(mod_summed, job + 1)
                if not first:
                    act.wait_ge(mod_stored, job * 16)
                for h in range(2):
                    act.activation(mod_out[32 * h:32 * h + 1, :], psum[32 * h:32 * h + 1, 6, :], copy).then_inc(mod_taken, 1)
                act.wait_ge(mod_taken, job * 2 + 2)
                act.dma_start(mod_rows[ds(job, 1), :].rearrange("a (h n) -> (a h) n", h=2), mod_out[0:33:32, :]
                              ).then_inc(mod_stored, 16)

            def turn(inst, m, dst=uT):
                if m is not None:
                    act.wait_ge(cols_ready, m + 1)
                for b in range(2):
                    act.wait_ge(tr_pe, inst * 4 + (b + 1))
                    for q in range(2):
                        kc = 2 * b + q
                        src = psum[:, 4 + b, S * q:S * q + S]
                        if m is None:
                            ins = act.activation(dst[:, kc, :], src, copy)
                        else:
                            ins = act.activation(dst[:, kc, :], src, copy, bias=shift_c[:, kc:kc + 1], scale=scale_c[:, kc:kc + 1])
                ins.then_inc(tr_act, 1)

            def norm(p):
                act.wait_ge(gated, p + 1)
                act.dma_start(gate_row[:, :], A["ln_b"][ds(p, 1), :].to_broadcast([P, D])).then_inc(lnb_landed, 16)
                act.wait_ge(pn_var, p + 1)
                act.activation(rstd[:, 0:TT], rstd[:, 0:TT], ACT.Sqrt).then_inc(pn_sqrt, 1)

            def ffn(l, k):
                f0 = 1 + l * (2 * TILES) + k * TILES

                def silu(t, i=0):
                    act.wait_ge(pe_gu, f0 + i * 4 + (t + 1))
                    if t >= 1:
                        act.wait_ge(dve_h, f0 + i * 4 + (t - 1))
                    act.activation(silu_g[:, t % 2, :], psum[:, 4 + t % 2, 0:S], ACT.Silu).then_inc(act_silu, 1)
                silu(0)
                with act.Fori(0, PAIRS) as i:
                    for t in range(1, 5):
                        silu(t, i)
                        if k == 0 and t % 2 == 0:
                            mod_row(l * JOBS_LAYER + i * 2 + (FIRST_JOBS + t // 2 - 1))
                        if k == 1 and t == 4:
                            mod_row(l * JOBS_LAYER + i + (FIRST_JOBS + JOBS_1))
                silu(TILES - 1)

            def mixer(l):
                act.wait_ge(mod_stored, (l * JOBS_LAYER + (FIRST_JOBS + JOBS_1)) * 16)
                for n in range(12):
                    act.wait_ge(m_pe.s, m_pe.at(f"proj{n}", l))
                    act.activation(proj[:, n % 2, 512 * (n // 2):512 * (n // 2) + 512], psum[:, 4 + n % 4, :], copy
                                   ).then_inc(m_act.sig(f"ev{n}"), 1)
                act.drain()
                act.activation(proj[:, :, RG:RG + 512], proj[:, :, RG:RG + 512], ACT.Silu).then_inc(m_act.sig("silu_g"), 1)
                for g in (0, 2, 4):
                    kind, hb = g // 2, g % 2
                    bk = psum[:, 4 + g % 4, :]
                    act.wait_ge(m_pe.s, m_pe.at(f"qk{g}", l))
                    for hh in range(2):
                        rows_ = slice(64 * hh, 64 * hh + 64)
                        act.activation(qm[rows_, NH * kind + 2 * hb + hh, :], bk[rows_, 0:S], copy)
                    act.activation(kT[:, 2 * kind + hb, :], bk[:, S:2 * S], copy).then_inc(m_act.sig(f"qk{g}"), 1)

                def exps(b):
                    act.wait_ge(m_dve.s, m_dve.at(f"max{b}", l))
                    for hh in range(2):
                        for t in range(TT):
                            blk = att[b % 2][:, hh, 0:P] if t == 0 else att[b % 2][:, hh, P:3 * P]
                            ins = act.activation(blk, blk, ACT.Exp, bias=neg_max[:, b // 2, 2 * hh + t:2 * hh + t + 1])
                    ins.then_inc(m_act.sig(f"exp{b}"), 1)

                def logs(b):
                    act.wait_ge(m_dve.s, m_dve.at(f"na{b}", l))
                    act.activation(stb_l, stb_l, ACT.Exp)
                    act.drain()
                    act.activation(stb_l, stb_l, ACT.Ln, bias=K["ones"][:, 0:1]).then_inc(m_act.sig(f"ln{b}"), 1)

                def p_turned(b):
                    act.wait_ge(m_pe.s, m_pe.at(f"B{b}", l))
                    act.activation(dil_pT, psum[:, 4 + 2 * (b % 2):6 + 2 * (b % 2), 0:3 * P], copy
                                   ).then_inc(m_act.sig(f"PT{b}"), 1)

                def stick(b):
                    act.wait_ge(m_dve.s, m_dve.at(f"s{b}", l))
                    act.activation(att[b % 2], att[b % 2], ACT.Exp).then_inc(m_act.sig(f"a{b}"), 1)

                exps(0)
                logs(1)
                p_turned(0)
                exps(2)
                stick(1)
                p_turned(2)
                logs(3)
                stick(3)
                act.wait_ge(m_dve.s, m_dve.at("gn_var", l))
                act.activation(rstd[:, :], rstd[:, :], ACT.Sqrt).then_inc(m_act.sig("gn_sqrt"), 1)
                turn(l * 4 + 2, None)

            act.wait_ge(s_const, 16 * (len(CONSTS) + 1))
            act.activation(cvec[:, 1, :, :], cvec[:, 0, :, :], ACT.Sigmoid).then_inc(cond_sig, 1)
            act.wait_ge(zeroed, 3)
            for job in range(FIRST_JOBS):
                mod_row(job, job == 0)
            with act.Fori(0, LAYERS) as l:
                turn(l * 4, l * 3)
                ffn(l, 0)
                norm(l * 3)
                turn(l * 4 + 1, l * 3 + 1)
                mixer(l)
                norm(l * 3 + 1)
                turn(l * 4 + 3, l * 3 + 2)
                ffn(l, 1)
                norm(l * 3 + 2)

            turn(8, 6)
            turn(9, 7, ctx_uT)
            for t in range(TT):
                act.wait_ge(m2_pe.s, m2_pe.at(f"c{t}"))
                act.activation(ctx_kv[:, t, :], psum[:, 6 + t, 0:256], copy).then_inc(m2_act.sig(f"c{t}"), 1)
            for t in range(TT):
                for b in range(3):
                    w = 512 if b < 2 else 256
                    act.wait_ge(m2_pe.s, m2_pe.at(f"p{t}{b}"))
                    act.activation(proj2[:, t, 512 * b:512 * b + w], psum[:, 3 * t + b, 0:w], copy
                                   ).then_inc(m2_act.sig(f"p{t}{b}"), 1)
            for i in range(2):
                act.wait_ge(m2_pe.s, m2_pe.at(f"grp{i}"))
                for g in (2 * i, 2 * i + 1):
                    ins = act.activation(uT[:, 4 + g, :], psum[:, 2 + i, S * (g % 2):S * (g % 2) + S], copy, scale=p_scale[:, g:g + 1])
                ins.then_inc(m2_act.sig(f"grp{i}"), 1)
            act.wait_ge(m2_dve.s, m2_dve.at("sq"))
            act.activation(stats[:, 0:4, :], stats[:, 0:4, :], ACT.Sqrt).then_inc(m2_act.sig("rms"), 1)
            act.wait_ge(m2_pe.s, m2_pe.at("kT"))
            act.activation(kT2[:, :], psum[:, 4, :], copy).then_inc(m2_act.sig("kT"), 1)
            act.wait_ge(m2_pe.s, m2_pe.at("q"))
            for j in (2, 3):
                for g in range(2):
                    rows_ = slice(64 * g, 64 * g + 64)
                    ins = act.activation(qm[rows_, 2 * j + g, :], psum[rows_, 6, S * (j % 2):S * (j % 2) + S], copy)
            ins.then_inc(m2_act.sig("q"), 1)
            for n in range(16):
                act.wait_ge(m2_dve.s, m2_dve.at(f"max{n}"))
                act.activation(prob[:, n % 2, :], psum[:, 4 + n % 2, :], ACT.Exp, bias=key_max[:, n:n + 1], scale=HD ** -0.5,
                               accum_out=den[:, n:n + 1]).then_inc(m2_act.sig(f"e{n}"), 1)
                act.wait_ge(m2_pe.s, m2_pe.at(f"T{n}"))
                act.activation(probT[:, n % 2, :], psum[:, 6 + n % 2, :], copy).then_inc(m2_act.sig(f"PT{n}"), 1)
            act.wait_ge(m2_pe.s, m2_pe.at("yT0"))
            act.activation(uT[:, 0:2, :], part(psum[:, 4, :], 0, 2, S), copy).then_inc(m2_act.sig("yT0"), 1)
            norm(6)

            def experts(layer):
                act.wait_ge(r_dve.s, r_dve.at("max", layer))
                for t in range(TT):
                    ins = act.activation(routeT[:, t, EXPERTS:2 * EXPERTS], psum[:, 4, EXPERTS * t:EXPERTS * t + EXPERTS], ACT.Exp,
                                         bias=neg_max[:, 0, t:t + 1], accum_out=den[:, t:t + 1])
                ins.then_inc(r_act.sig("exp"), 1)
                for kc in (0, 2, 4, 6):
                    act.wait_ge(r_pe.s, r_pe.at(f"g{kc}", layer))
                    act.activation(xeT[:, kc, :], psum[:, kc, :], copy, bias=shift_c[:, kc:kc + 1], scale=scale_c[:, kc:kc + 1]
                                   ).then_inc(r_act.sig(f"g{kc}"), 1)
                with act.Fori(0, EXPERTS) as e:
                    E = e + EXPERTS * layer
                    act.wait_ge(e_pe.s, e_pe.at("k7", E))
                    act.activation(e_silu[:, :], psum[:, 4, 0:256], ACT.Silu).then_inc(e_act.sig("silu"), 1)
                    act.wait_ge(e_pe.s, e_pe.at("hT", E))
                    act.activation(e_hT[:, :, :], part(psum[:, 5, :], 0, 4, P)[:, 0:2, :], copy).then_inc(e_act.sig("hT"), 1)
                    act.wait_ge(e_pe.s, e_pe.at("d3", E))
                    for q in range(2):
                        ins = act.activation(R[32 * q:32 * q + 32, 256 * q:256 * q + 256], psum[32 * q:32 * q + 32, 6, 0:256], copy)
                    ins.then_inc(e_act.sig("R"), 1)
            turn(10, 8)
            experts(0)
            norm(7)
            turn(11, 9)
            for fb in range(KC):
                act.wait_ge(cv_pe.s, cv_pe.at(f"f{fb}"))
                if fb >= 2:
                    act.wait_ge(cv_dve.s, cv_dve.at(f"f{fb - 2}"))
                bk = psum[:, 4 + 2 * (fb % 2), :]
                act.activation(conv_c[:, fb % 2, :], bk[:, S:2 * S], copy)
                act.activation(conv_b[:, fb % 2, :], bk[:, 0:S], copy).then_inc(cv_act.sig(f"f{fb}"), 1)
            norm(8)
            turn(12, 10)
            experts(1)
            norm(9)

        @block.vector
        def _(dve):
            mul, add, sub = ALU.mult, ALU.add, ALU.subtract

            def mod_part(job, c, first=False):
                if c == 0:
                    dve.tensor_copy(cond_now[:, :], cond[:, ds(job, 1), :].rearrange("p a k -> p (a k)"))
                    dve.drain()
                    dve.wait_ge(bias_landed, job * 16 + 16)
                    if not first:
                        dve.wait_ge(mod_summed, job)
                dve.wait_ge(mod_landed[c % 2], job * 32 + 16 * (c // 2 + 1))
                for kk in range(2):
                    kc = 2 * c + kk
                    w = part(W_mod[:, c % 2, :], 0, 2, D)[:, kk, :]
                    ins = dve.scalar_tensor_tensor(mod_acc[:, :], w, cond_now[:, kc:kc + 1], mod_bias[:, :] if kc == 0 else mod_acc[:, :],
                                                   mul, add)
                    if kk == 0:
                        if kc == 0:
                            ins.then_inc(cond_read, 1)
                        dve.drain()
                ins.then_inc(mod_freed[c % 2], 1)
                dve.drain()
                if c == 3:
                    dve.engine_nop().then_inc(mod_ready, 1)

            def columns(m):
                dve.wait_ge(cols_landed, m * 32 + 32)
                dve.tensor_scalar(scale_c[:, :], scale_c[:, :], 1.0, None, add).then_inc(cols_ready, 1)
                dve.drain()

            def turn(inst, m, dst=uT):
                if m is not None:
                    columns(m)
                for b in (2, 3):
                    dve.wait_ge(tr_pe, inst * 4 + (b + 1))
                    for q in range(2):
                        kc = 2 * b + q
                        src = psum[:, 4 + b, S * q:S * q + S]
                        if m is None:
                            ins = dve.tensor_copy(dst[:, kc, :], src)
                        else:
                            ins = dve.tensor_scalar(dst[:, kc, :], src, scale_c[:, kc:kc + 1], shift_c[:, kc:kc + 1], mul, add)
                ins.then_inc(tr_dve, 1)

            def norm(p, acc, alpha, res, eps):
                dve.wait_ge(rows_landed, p * 32 + 32)
                if res is not None:
                    dve.tensor_scalar(gate_row[:, :], gate_row[:, :], 1.0, res, add, mul)
                    dve.drain()
                dve.wait_ge(*acc)
                for t in range(TT):
                    ins = dve.tensor_tensor(part(tmp[:, t, :], 0, 2, 512), psum[:, 2 * t:2 * t + 2, :], part(gate_row[:, :], 0, 2, 512), mul)
                ins.then_inc(gated, 1)
                dve.drain()
                for t in range(TT):
                    dve.scalar_tensor_tensor(tmp[:, t, :], x_tok[:, t, :], alpha, tmp[:, t, :], mul, add)
                dve.drain()
                for t in range(TT):
                    for h in range(2):
                        dve.bn_stats(stats[:, 2 * t + h, :], tmp[:, t, 512 * h:512 * h + 512])
                dve.drain()
                for t in range(TT):
                    dve.bn_aggr(mv[:, t, :], stats[:, 2 * t:2 * t + 2, :])
                dve.drain()
                dve.tensor_scalar(rstd[:, 0:TT], mv[:, 0:TT, 1], eps, None, add).then_inc(pn_var, 1)
                for t in range(TT):
                    dve.scalar_tensor_tensor(tmp[:, t, :], tmp[:, t, :], mv[:, t, 0:1], gain_row[:, :], sub, mul)
                dve.wait_ge(pn_sqrt, p + 1)
                dve.reciprocal(rstd[:, 0:TT], rstd[:, 0:TT])
                dve.drain()
                dve.wait_ge(lnb_landed, p * 16 + 16)
                for t in range(TT):
                    dve.scalar_tensor_tensor(x_tok[:, t, :], tmp[:, t, :], rstd[:, t:t + 1], gate_row[:, :], mul, add
                                             ).then_inc(pn_x, 1)

            def ffn(l, k):
                f0 = 1 + l * (2 * TILES) + k * TILES

                def hidden(t, i=0):
                    dve.wait_ge(act_silu, f0 + i * 4 + (t + 1))
                    if t >= 1:
                        dve.wait_ge(pe_down, f0 + i * 4 + (t - 1))
                    dve.tensor_tensor(hT[:, t % 2, :], silu_g[:, t % 2, :], psum[:, 4 + t % 2, S:2 * S], mul).then_inc(dve_h, 1)
                hidden(0)
                with dve.Fori(0, PAIRS) as i:
                    for t in range(1, 5):
                        hidden(t, i)
                        if k == 0:
                            for c in ((2, 3) if t % 2 == 0 else (0, 1)):
                                mod_part(l * JOBS_LAYER + i * 2 + (FIRST_JOBS + (t - 1) // 2), c)
                        else:
                            mod_part(l * JOBS_LAYER + i + (FIRST_JOBS + JOBS_1), t - 1)
                hidden(TILES - 1)

            def rotate(l, kind, table):
                for t in range(TT):
                    if t:
                        dve.drain()
                    x = proj[:, t, QCOL[kind]:QCOL[kind] + 512]
                    x4, a4, b4 = (part(v, 0, 2 * NH, 2, 32) for v in (x, rope_a, rope_b))
                    c_, s_ = (K["rope1"][:, 2 * table + n, t, :] for n in range(2))
                    dve.tensor_tensor(a4, x4, c_.unsqueeze(1).unsqueeze(1).to_broadcast([P, 2 * NH, 2, 32]), mul)
                    s8 = s_.unsqueeze(1).to_broadcast([P, 2 * NH, 32])
                    for n in range(2):
                        dve.tensor_tensor(b4[:, :, n, :], x4[:, :, 1 - n, :], s8, mul)
                    dve.drain()
                    dve.tensor_tensor(x4[:, :, 0, :], a4[:, :, 0, :], b4[:, :, 0, :], sub)
                    ins = dve.tensor_tensor(x4[:, :, 1, :], a4[:, :, 1, :], b4[:, :, 1, :], add)
                ins.then_inc(m_dve.sig(f"rot{table}"), 1)

            def mixer(l):
                for table, (kind, group) in enumerate(((RET, 0), (DIL, 3))):
                    dve.drain()
                    dve.wait_ge(m_act.s, m_act.at(f"ev{2 * group + 1}", l))
                    rotate(l, kind, table)
                for g in (1, 3, 5):
                    kind, hb = g // 2, g % 2
                    bk = psum[:, 4 + g % 4, :]
                    dve.wait_ge(m_pe.s, m_pe.at(f"qk{g}", l))
                    for hh in range(2):
                        rows_ = slice(64 * hh, 64 * hh + 64)
                        dve.tensor_copy(qm[rows_, NH * kind + 2 * hb + hh, :], bk[rows_, 0:S])
                    dve.tensor_copy(kT[:, 2 * kind + hb, :], bk[:, S:2 * S]).then_inc(m_dve.sig(f"qk{g}"), 1)

                def pair(b):
                    return psum[:, 4 + 2 * (b % 2):6 + 2 * (b % 2), 0:3 * P]

                def both(x, n):
                    return x.unsqueeze(1).to_broadcast([P, 2, n])

                def maxima(b):
                    dve.wait_ge(m_pe.s, m_pe.at(f"A{b}", l))
                    a, closed = att[b % 2], K["closed"]
                    dve.scalar_tensor_tensor(a[:, :, 0:P], pair(b)[:, :, 0:P], HD ** -0.5, both(closed[:, P:S], P), mul, add)
                    dve.scalar_tensor_tensor(a[:, :, P:3 * P], pair(b)[:, :, P:3 * P], HD ** -0.5, both(closed[:, :], S), mul, add)
                    dve.drain()
                    m = part(neg_max[:, b // 2, :], 0, 2, 2)
                    dve.tensor_reduce(m[:, :, 0], a[:, :, 0:P], AX_X, ALU.max, negate=True)
                    dve.tensor_reduce(m[:, :, 1], a[:, :, P:3 * P], AX_X, ALU.max, negate=True).then_inc(m_dve.sig(f"max{b}"), 1)

                def weighted(b):
                    dve.wait_ge(m_act.s, m_act.at(f"exp{b}", l))
                    for hh in range(2):
                        a, d = att[b % 2][:, hh, :], den[:, 4 * (b // 2) + 2 * hh:4 * (b // 2) + 2 * hh + 2]
                        dve.scalar_tensor_tensor(a[:, 0:P], a[:, 0:P], 1.0, K["windows"][:, P:S], mul, mul, accum_out=d[:, 0:1])
                        ins = dve.scalar_tensor_tensor(a[:, P:3 * P], a[:, P:3 * P], 1.0, K["windows"][:, :], mul, mul,
                                                       accum_out=d[:, 1:2])
                    ins.then_inc(m_dve.sig(f"p{b}"), 1)

                def dil_out(b):
                    dve.wait_ge(m_pe.s, m_pe.at(f"C{b}", l))
                    d = den[:, 4 * (b // 2):4 * (b // 2) + 4]
                    dve.reciprocal(d, d)
                    dve.drain()
                    for hh in range(2):
                        for t in range(TT):
                            h = 2 * (b // 2) + hh
                            ins = dve.tensor_scalar(y_tok[:, t, 512 + HD * h:512 + HD * h + HD], psum[:, 2, S * t + HD * h:S * t + HD * h + HD],
                                                    d[:, 2 * hh + t:2 * hh + t + 1], None, mul)
                    ins.then_inc(m_dve.sig(f"y{b}"), 1)

                def neg_abs(b):
                    dve.wait_ge(m_pe.s, m_pe.at(f"A{b}", l))
                    dve.tensor_scalar(stb_z, pair(b), HD ** -0.5, None, mul)
                    dve.drain()
                    dve.scalar_tensor_tensor(stb_l, stb_z, -1.0, stb_z, mul, ALU.min).then_inc(m_dve.sig(f"na{b}"), 1)

                def mask_own(x):
                    dve.tensor_tensor(x[:, :, 0:P], x[:, :, 0:P], both(K["strict"][:, :], P), mul)
                    return dve.tensor_tensor(x[:, :, S:3 * P], x[:, :, S:3 * P], both(K["strict"][:, :], P), mul)

                def keeps(b):
                    dve.wait_ge(m_act.s, m_act.at(f"ln{b}", l))
                    dve.scalar_tensor_tensor(att[b % 2], stb_z, 0.0, stb_l, ALU.min, sub)
                    dve.drain()
                    dve.tensor_tensor(stb_z, att[b % 2], stb_z, sub)
                    dve.drain()
                    mask_own(stb_z).then_inc(m_dve.sig(f"lk{b}"), 1)

                def sticks(b):
                    dve.wait_ge(m_pe.s, m_pe.at(f"B{b}", l))
                    dve.tensor_tensor(att[b % 2], att[b % 2], pair(b), add).then_inc(m_dve.sig(f"s{b}"), 1)

                def stick_mask(b):
                    dve.wait_ge(m_act.s, m_act.at(f"a{b}", l))
                    mask_own(att[b % 2]).then_inc(m_dve.sig(f"am{b}"), 1)

                def stick_out(b):
                    dve.wait_ge(m_pe.s, m_pe.at(f"C{b}", l))
                    c = P * (b // 2)
                    dve.tensor_copy(y_tok[:, :, 768 + c:768 + c + P], part(psum[:, 3, :], 0, TT, S)[:, :, c:c + P]
                                    ).then_inc(m_dve.sig(f"y{b}"), 1)

                def decayed(b):
                    dve.wait_ge(m_pe.s, m_pe.at(f"A{b}", l))
                    h = 2 * ATT[b][1]
                    dve.tensor_tensor(att[b % 2][:, :, 0:S], pair(b)[:, :, 0:S], K["decay"][:, h:h + 2, :], mul)
                    dve.tensor_tensor(att[b % 2][:, :, S:3 * P], pair(b)[:, :, S:3 * P], K["decay"][:, h:h + 2, 0:P], mul
                                      ).then_inc(m_dve.sig(f"r{b}"), 1)

                maxima(0)
                neg_abs(1)
                weighted(0)
                keeps(1)
                maxima(2)
                dil_out(0)
                sticks(1)
                stick_mask(1)
                weighted(2)
                neg_abs(3)
                stick_out(1)
                keeps(3)
                dil_out(2)
                sticks(3)
                decayed(4)
                stick_mask(3)
                decayed(5)
                stick_out(3)
                dve.wait_ge(m_pe.s, m_pe.at("C5", l))
                for t in range(TT):
                    for h in range(NH):
                        dve.bn_stats(stats[:, NH * t + h, :], psum[:, t, RDV * h:RDV * h + RDV])
                dve.drain()
                for n in range(2 * NH):
                    dve.bn_aggr(mv[:, n, :], stats[:, n, :])
                dve.drain()
                dve.tensor_scalar(rstd[:, :], mv[:, :, 1], GN_EPS, None, add).then_inc(m_dve.sig("gn_var"), 1)
                dve.wait_ge(m_act.s, m_act.at("gn_sqrt", l))
                dve.reciprocal(rstd[:, :], rstd[:, :])
                dve.drain()
                for t in range(TT):
                    for h in range(NH):
                        n = NH * t + h
                        dve.tensor_scalar(y_tok[:, t, RDV * h:RDV * h + RDV], psum[:, t, RDV * h:RDV * h + RDV],
                                          mv[:, n, 0:1], rstd[:, n:n + 1], sub, mul)
                dve.drain()
                dve.wait_ge(m_act.s, m_act.at("silu_g", l))
                dve.tensor_tensor(y_tok[:, :, 0:512], y_tok[:, :, 0:512], proj[:, :, RG:RG + 512], mul).then_inc(m_dve.sig("y"), 1)
                turn(l * 4 + 2, None)

            for sem_ in (pe_gu, pe_down, act_silu, dve_h, tr_act, tr_dve):
                dve.engine_nop().then_inc(sem_, 1)
            dve.wait_ge(s_x, 16)
            dve.engine_nop().then_inc(pn_x, 2)
            dve.wait_ge(cond_sig, 1)
            dve.tensor_tensor(cvec[:, 0, :, :], cvec[:, 0, :, :], cvec[:, 1, :, :], mul)
            dve.drain()
            for n, (a, b) in enumerate(((0, MOD2), (MOD2, CTX_ROW), (CTX_ROW, JOBS))):
                dve.tensor_copy(cond[:, a:b, :], cvec[:, 0, n, :].unsqueeze(1).to_broadcast([P, b - a, KC]))
            dve.drain()
            for job in range(FIRST_JOBS):
                for c in range(4):
                    mod_part(job, c, job == 0)
            with dve.Fori(0, LAYERS) as l:
                turn(l * 4, l * 3)
                ffn(l, 0)
                norm(l * 3, (pe_down, l * (2 * TILES) + (1 + TILES)), ALPHA, 0.5, LN_EPS)
                turn(l * 4 + 1, l * 3 + 1)
                mixer(l)
                norm(l * 3 + 1, (m_pe.s, m_pe.at("out", l)), ALPHA, 1.0, LN_EPS)
                turn(l * 4 + 3, l * 3 + 2)
                ffn(l, 1)
                norm(l * 3 + 2, (pe_down, l * (2 * TILES) + (1 + 2 * TILES)), ALPHA, 0.5, LN_EPS)

            turn(8, 6)
            turn(9, 7, ctx_uT)
            dve.wait_ge(s_const2, 16 * (len(CONSTS2) + 1))
            for i in range(2):
                dve.wait_ge(m2_pe.s, m2_pe.at(f"pool{i}"))
                dve.tensor_copy(pooledT[:, 2 * i:2 * i + 2, :], part(psum[:, 2 + i, :], 0, 2, S)).then_inc(m2_dve.sig(f"pool{i}"), 1)
            ms = part(stats[:, 0:4, :].rearrange("p a b -> p (a b)"), 0, TT, 12)
            for t in range(TT):
                dve.tensor_tensor(squares[:, t, 0:640], proj2[:, t, 0:640], proj2[:, t, 0:640], mul)
                dve.tensor_tensor(squares[:, t, 640:768], ctx_kv[:, t, 0:P], ctx_kv[:, t, 0:P], mul)
            dve.drain()
            for t in range(TT):
                dve.tensor_reduce(ms[:, t, :], part(squares[:, t, :], 0, 12, HD), AX_X, add)
            dve.drain()
            dve.tensor_scalar(ms, ms, 1.0 / HD, NORM_EPS, mul, add).then_inc(m2_dve.sig("sq"), 1)
            dve.wait_ge(m2_act.s, m2_act.at("rms"))
            dve.reciprocal(ms, ms)
            dve.drain()
            heads = [(part(proj2[:, t, 0:512], 0, 8, HD), t, 0, 8, 0) for t in range(TT)]
            heads += [(part(proj2[:, t, 512:640], 0, 2, HD), t, 8, 2, 1) for t in range(TT)]
            heads += [(part(ctx_kv[:, t, 0:P], 0, 2, HD), t, 10, 2, 1) for t in range(TT)]
            for x, t, h0, n, _ in heads:
                dve.tensor_tensor(x, x, ms[:, t, h0:h0 + n].unsqueeze(2).to_broadcast([P, n, HD]), mul)
            dve.drain()
            for x, _, _, n, g in heads:
                dve.tensor_tensor(x, x, qk_gain[:, g, :].unsqueeze(1).to_broadcast([P, n, HD]), mul)
            dve.drain()
            for t in range(TT):
                if t:
                    dve.drain()
                x, a, b = (part(v, 0, 10, 32, 2) for v in (proj2[:, t, 0:640], tmp[:, 0, 0:640], tmp[:, 1, 0:640]))
                c_, s_ = rope2[:, 0, t, :], rope2[:, 1, t, :]
                dve.tensor_tensor(a, x, c_.unsqueeze(1).unsqueeze(3).to_broadcast([P, 10, 32, 2]), mul)
                s10 = s_.unsqueeze(1).to_broadcast([P, 10, 32])
                for n in range(2):
                    dve.tensor_tensor(b[:, :, :, n], x[:, :, :, 1 - n], s10, mul)
                dve.drain()
                dve.tensor_tensor(x[:, :, :, 0], a[:, :, :, 0], b[:, :, :, 0], sub)
                ins = dve.tensor_tensor(x[:, :, :, 1], a[:, :, :, 1], b[:, :, :, 1], add)
            ins.then_inc(m2_dve.sig("rope"), 1)
            dve.wait_ge(m2_pe.s, m2_pe.at("q"))
            for j in (0, 1):
                for g in range(2):
                    rows_ = slice(64 * g, 64 * g + 64)
                    ins = dve.tensor_copy(qm[rows_, 2 * j + g, :], psum[rows_, 5, S * j:S * j + S])
            ins.then_inc(m2_dve.sig("q"), 1)
            for n in range(16):
                dve.wait_ge(m2_pe.s, m2_pe.at(f"S{n}"))
                dve.tensor_reduce(key_max[:, n:n + 1], psum[:, 4 + n % 2, :], AX_X, ALU.max, negate=True)
                dve.drain()
                dve.tensor_scalar(key_max[:, n:n + 1], key_max[:, n:n + 1], HD ** -0.5, None, mul).then_inc(m2_dve.sig(f"max{n}"), 1)
            dve.wait_ge(m2_pe.s, m2_pe.at("V15"))
            dve.reciprocal(den[:, :], den[:, :])
            dve.drain()
            for t in range(TT):
                d = den[:, :].rearrange("p (h t) -> p t h", t=2)[:, t, :]
                ins = dve.tensor_tensor(part(proj2[:, t, 0:512], 0, 8, HD), part(psum[:, t, :], 0, 8, HD),
                                        d.unsqueeze(2).to_broadcast([P, 8, HD]), mul)
            ins.then_inc(m2_dve.sig("y"), 1)
            dve.wait_ge(m2_pe.s, m2_pe.at("yT1"))
            dve.tensor_copy(uT[:, 2:4, :], part(psum[:, 5, :], 0, 2, S)).then_inc(m2_dve.sig("yT1"), 1)
            norm(6, (m2_pe.s, m2_pe.at("out")), ALPHA, None, NORM_EPS)

            def experts(layer):
                X = slice(0, EXPERTS)
                dve.wait_ge(r_pe.s, r_pe.at("logits", layer))
                dve.tensor_reduce(neg_max[:, 0, 0:TT], part(psum[:, 4, :], 0, 32, EXPERTS)[:, 0:TT, :], AX_X, ALU.max, negate=True
                                  ).then_inc(r_dve.sig("max"), 1)
                dve.memset(R[:, :], 0.0)
                dve.wait_ge(r_act.s, r_act.at("exp", layer))
                dve.reciprocal(den[:, 0:TT], den[:, 0:TT])
                dve.drain()
                gates = routeT[:, :, EXPERTS:2 * EXPERTS]
                dve.tensor_tensor(gates, gates, den[:, 0:TT].unsqueeze(2).to_broadcast([P, TT, EXPERTS]), mul
                                  ).then_inc(r_dve.sig("aff"), 1)
                dve.wait_ge(r_pe.s, r_pe.at("affT", layer))
                dve.tensor_copy(route[X, 0, :], psum[X, 5, 0:S])
                dve.drain()
                src, dst = route[X, 0, :], route[X, 1, :]
                for r in range(CAP // 8):
                    dve.max(top8[X, :], src)
                    dve.drain()
                    dve.match_replace(dst, top8[X, :], src, -1.0)
                    dve.drain()
                    src, dst = dst, route[X, 1 + (r + 1) % 2, :]
                dve.tensor_scalar(route[X, 1, :], src, 0.0, None, ALU.is_lt)
                dve.drain()
                dve.tensor_tensor_scan(route[X, 3, :], route[X, 1, :], route[X, 1, :], 0.0, add, ALU.max)
                dve.drain()
                dve.tensor_tensor(route[X, 3, :], route[X, 3, :], route[X, 1, :], mul).then_inc(r_dve.sig("slot"), 1)
                dve.wait_ge(r_pe.s, r_pe.at("slotT", layer))
                dve.tensor_copy(routeT[:, :, 0:EXPERTS], part(psum[:, 5, :], 0, 32, EXPERTS)[:, 0:TT, :])
                dve.drain()
                for t in range(TT):
                    ins = dve.tensor_tensor(part(sel[:, t, :], 0, EXPERTS, CAP), routeT[:, t, X].unsqueeze(2).to_broadcast([P, EXPERTS, CAP]),
                                            slot_no[:, 0:CAP].unsqueeze(1).to_broadcast([P, EXPERTS, CAP]), ALU.is_equal)
                ins.then_inc(r_dve.sig("sel"), 1)
                for kc in (1, 3, 5, 7):
                    dve.wait_ge(r_pe.s, r_pe.at(f"g{kc}", layer))
                    dve.tensor_scalar(xeT[:, kc, :], psum[:, kc, :], scale_c[:, kc:kc + 1], shift_c[:, kc:kc + 1], mul, add
                                      ).then_inc(r_dve.sig(f"g{kc}"), 1)
                dve.wait_ge(r_act.s, r_act.at("g6", layer))
                dve.drain()
                with dve.Fori(0, EXPERTS) as e:
                    E = e + EXPERTS * layer
                    dve.tensor_copy(xe_now[:, :, :], xeT[:, :, ds(e * CAP, CAP)])
                    for t in range(TT):
                        ins = dve.tensor_scalar(G_now[:, t, :], slot_no[:, :], routeT[:, t, ds(e, 1)], routeT[:, t, ds(e + EXPERTS, 1)],
                                                ALU.is_equal, mul)
                    ins.then_inc(e_dve.sig("xG"), 1)
                    dve.wait_ge(e_act.s, e_act.at("silu", E))
                    dve.tensor_tensor(e_h[:, :], e_silu[:, :], psum[:, 4, 256:512], mul).then_inc(e_dve.sig("h"), 1)
                    dve.wait_ge(e_pe.s, e_pe.at("gT", E))
                    dve.tensor_copy(GT[:, :], psum[:, 7, 0:S]).then_inc(e_dve.sig("gT"), 1)
                    dve.wait_ge(e_pe.s, e_pe.at("d3", E))
                    for q in (2, 3):
                        ins = dve.tensor_copy(R[32 * q:32 * q + 32, 256 * q:256 * q + 256], psum[32 * q:32 * q + 32, 6, 0:256])
                    ins.then_inc(e_dve.sig("R"), 1)
            turn(10, 8)
            experts(0)
            norm(7, (e_pe.s, e_pe.at("out", EXPERTS - 1)), ALPHA, None, NORM_EPS)
            turn(11, 9)
            dve.memset(conv_s[:, :, 0:S + 2:S + 1], 0.0)
            dve.drain()
            for fb in range(KC):
                q = fb % 2
                dve.wait_ge(cv_act.s, cv_act.at(f"f{fb}"))
                dve.tensor_tensor(conv_s[:, q, 1:S + 1], conv_c[:, q, :], psum[:, 5 + 2 * q, 0:S], mul)
                dve.drain()
                dve.tensor_scalar(conv_z[:, q, :], conv_s[:, q, 0:S], conv_w[:, fb, 0:1], None, mul)
                for j in (1, 2):
                    dve.drain()
                    dve.scalar_tensor_tensor(conv_z[:, q, :], conv_s[:, q, j:j + S], conv_w[:, fb, j:j + 1], conv_z[:, q, :], mul, add)
                dve.drain()
                dve.tensor_tensor(conv_yT[:, fb, :], conv_z[:, q, :], conv_b[:, q, :], mul).then_inc(cv_dve.sig(f"f{fb}"), 1)
            norm(8, (cv_pe.s, cv_pe.at("out")), ALPHA, None, NORM_EPS)
            turn(12, 10)
            experts(1)
            norm(9, (e_pe.s, e_pe.at("out", 2 * EXPERTS - 1)), ALPHA, None, NORM_EPS)


def kernel(**inputs):
    import concourse.bacc as bacc
    from concourse.bass_utils import run_bass_kernel_spmd as run

    def cols(v):
        v = np.asarray(v)
        return np.ascontiguousarray(np.moveaxis(v.reshape(v.shape[:-1] + (KC, P)), -1, 0))
    g = {k: np.asarray(v) for k, v in inputs.items()}
    a = {n: g[n] for n in ("ffn1_w_gate", "ffn1_w_up", "ffn1_w_down", "w_in", "w_out",
                           "ffn2_w_gate", "ffn2_w_up", "ffn2_w_down")}
    a["x"], a["ctx"] = g["x"][0], g["ctx_2"][0]
    q_cols = np.arange(QH * HD).reshape(2, QH // 2, HD).transpose(1, 0, 2).ravel()
    a["w_mix_in"] = g["w_mix_in_2"][0][:, np.concatenate([q_cols, np.arange(QH * HD, MIX2_W)])]
    a["w_mix_out"] = g["w_mix_out_2"][0]
    a["w_conv_in"], a["w_conv_out"] = g["w_conv_in_2"][0], g["w_conv_out_2"][0]
    a["w_exp_gate"], a["w_exp_up"], a["w_exp_down"] = g["w_exp_gate_2"], g["w_exp_up_2"], g["w_exp_down_2"]
    ada = g["w_ada"].reshape(LAYERS, D, 9, D).transpose(0, 2, 1, 3).reshape(MOD2, D, D)
    mod = g["w_mod_2"].reshape(LAYERS, D, 6, D).transpose(0, 2, 1, 3).reshape(12, D, D)
    a["mod_w"] = np.concatenate([ada, mod, mod[0:2]])
    mod_b = g["b_mod_2"].reshape(12, D)
    a["mod_b"] = np.concatenate([g["b_ada"].reshape(MOD2, D), mod_b, mod_b[0:2]])
    a["cvec"] = cols(np.stack([g["c"][0], g["c_2"][0], g["c_ctx_2"]]))
    a["ln_g"] = np.concatenate([g["ln_gain"].reshape(6, D), np.stack([g["ln_mix_g_2"], g["ln_ffn_g_2"]], 1).reshape(4, D)])
    a["ln_b"] = np.concatenate([g["ln_bias"].reshape(6, D), np.stack([g["ln_mix_b_2"], g["ln_ffn_b_2"]], 1).reshape(4, D)])
    a["w_grp"] = g["w_pool_grp_2"][0].transpose(1, 0, 2)
    a["qk_gain"] = np.tile(np.stack([g["q_norm_g_2"][0], g["k_norm_g_2"][0]])[None], (P, 1, 1))
    a["p_scale"] = g["pool_scale_2"][0].reshape(4, P).T
    a["w_router"] = g["w_router_2"].reshape(LAYERS, KC, P, EXPERTS).transpose(2, 0, 1, 3).reshape(P, LAYERS, KC * EXPERTS)
    a["conv_w"] = g["conv_w_2"][0].reshape(3, KC, P).transpose(2, 1, 0)
    a.update(stack_constants())
    a = {"in_" + k: np.ascontiguousarray(v) for k, v in a.items()}

    nc = bacc.Bacc("TRN2", target_bir_lowering=False, num_devices=1)
    aps = {k[3:]: nc.dram_tensor(k, v.shape, mybir.dt.from_np(v.dtype), kind="ExternalInput").ap() for k, v in a.items()}
    out = nc.dram_tensor("out", (S, D), F32, kind="ExternalOutput").ap()
    build(nc, aps, out)
    r = run(nc, [a], core_ids=[0])
    return r.results[0]["out"].reshape(1, S, D)
```

```python
from contextlib import ExitStack

import numpy as np

import concourse.bass as bass
from concourse import mybir

F32 = mybir.dt.float32
R32 = mybir.dt.float32r
ALU = mybir.AluOpType
ACT = mybir.ActivationFunctionType
AX_X = mybir.AxisListType.X

P = 128
S = 256
TT = S // P
D = 1024
KC = D // P
FF = 2816
TILES = FF // P
STEP = 2 * P
PAIRS = (TILES - 2) // 4
LAYERS = 2
HD = 64
RDV = 128
NH = 4
IN_W = 3072
MIX2_W = 1280
QH = 8
EXPERTS = 16
CAP = 2 * S // EXPERTS
NEG = -1.0e30
ALPHA = (2.0 * LAYERS) ** 0.25
LN_EPS, GN_EPS, NORM_EPS = 1e-5, 1e-6, 1e-6

RQ, RK, RV, RG, DQ, DK, DV, SQ, SK, SV = 0, 256, 512, 1024, 1536, 1792, 2048, 2304, 2560, 2816
RET, DIL, STB = 0, 1, 2
QCOL, KCOL, VCOL, VW = (RQ, DQ, SQ), (RK, DK, SK), (RV, DV, SV), (RDV, HD, HD)

MOD2 = 9 * LAYERS
CTX_ROW = MOD2 + 6 * LAYERS
JOBS = CTX_ROW + 2
FIRST_JOBS = 2
JOBS_LAYER = 3 * PAIRS
assert FIRST_JOBS + LAYERS * JOBS_LAYER == JOBS

MIX_S = (6, 7, 8, 9, 10, 11)
MIX_SLOTS = len(MIX_S)
MIX_IN_USES = IN_W * D // (P * 2048)
MIX_USES = MIX_IN_USES + D * D // (P * 2048)
PER_LAYER = [sum(1 for u in range(MIX_USES) if u % MIX_SLOTS == s) for s in range(MIX_SLOTS)]
SLOTS = 12

ATT = [(DIL, 0), (STB, 0), (DIL, 1), (STB, 1), (RET, 0), (RET, 1)]


class Steps:

    def __init__(self, sem, names):
        self.s, self.names, self.next = sem, list(names), 0

    def at(self, name, inst=0):
        return inst * len(self.names) + self.names.index(name) + 1

    def sig(self, name):
        assert self.names[self.next] == name, (self.names[self.next], name)
        self.next = (self.next + 1) % len(self.names)
        return self.s


def stack_constants():
    i = np.arange(P, dtype=np.float64)
    t = np.arange(S, dtype=np.float32)
    out = {}
    out["ident"] = np.eye(P, dtype=np.float32)
    out["ones"] = np.ones((P, P), np.float32)
    out["later"] = (i[:, None] > i[None, :]).astype(np.float32)
    out["strict"] = (i[:, None] < i[None, :]).astype(np.float32)
    lg = np.log1p(-np.exp2(-5.0 - np.arange(NH)))
    ret = np.zeros((P, NH, S))
    for h in range(NH):
        dist = np.arange(S)[None, :] - i[:, None]
        ret[:, h] = np.where(dist >= 0, np.exp(lg[h] * np.maximum(dist, 0)), 0.0) * HD ** -0.5
    out["decay"] = ret.astype(np.float32)
    dist = i[:, None] + P - np.arange(S)[None, :]
    cnt = np.zeros((P, S))
    for w, dl in zip((128, 512, 2048), (1, 4, 16)):
        cnt += (dist >= 0) & (dist % dl == 0) & (dist <= w)
    out["windows"] = cnt.astype(np.float32)
    out["closed"] = np.where(cnt > 0, 0.0, NEG).astype(np.float32)

    def rope(freq):
        ang = (t[:, None] * freq[None, :].astype(np.float32)).astype(np.float32).astype(np.float64)
        return np.cos(ang), np.sin(ang)

    def tiles(a):
        return a.reshape(TT, P, -1).transpose(1, 0, 2).astype(np.float32)
    f32 = np.float32
    rows = []
    for freq in (1.0 / f32(10000.0) ** np.linspace(0.0, 1.0, 32, dtype=f32),
                 1.0 / f32(10000.0) ** (np.arange(0, HD, 2, dtype=f32) / f32(HD))):
        c, s = rope(freq)
        rows += [tiles(c), tiles(s)]
    out["rope1"] = np.stack(rows, 1)
    f = f32(10000.0) ** (-np.arange(0, 32, 2, dtype=f32) / f32(32))
    row, col = np.repeat(np.arange(S // 64), 64).astype(f32), np.tile(np.arange(64), S // 64).astype(f32)
    ang = np.concatenate([(row[:, None] * f), (col[:, None] * f)], 1).astype(f32).astype(np.float64)
    out["rope2"] = np.stack([tiles(np.cos(ang)), tiles(np.sin(ang))], 1)
    out["slot_no"] = np.tile((np.arange(P) % CAP + 1).astype(np.float32), (P, 1))
    pool = np.zeros((4, S, S))
    for g, w in enumerate((2, 4, 8, 16)):
        for q in range(S):
            lo, hi = max(q - w // 2, 0), min(q + w // 2, S)
            pool[g, lo:hi, q] += 1.0 / (hi - lo)
            pool[g, q, q] -= 1.0
    out["pool"] = pool.reshape(4, TT, P, S).transpose(2, 0, 1, 3).astype(np.float32)
    return out



CONSTS = ("ident", "ones", "later", "strict", "decay", "windows", "closed", "rope1")
CONSTS2 = ("pool", "w_grp", "rope2", "qk_gain", "p_scale", "w_router", "conv_w", "slot_no")


def build(nc, A, out):
    with ExitStack() as ctx:
        def sb(name, shape):
            return ctx.enter_context(nc.sbuf_tensor(name, shape, F32))

        def sem(name):
            return ctx.enter_context(nc.semaphore(name))

        def steps(name, names):
            return Steps(sem(name), names)

        ds = bass.ds
        ctx.enter_context(nc.allow_non_contiguous_dma(reason="modulation rows are read as columns"))
        mod_rows = nc.dram_tensor("mod_rows", [JOBS, D], F32, kind="Internal").ap()

        SCR = 7680
        with nc.sbuf_tensor("below_parts", [P, 8, 2048], F32):
            with nc.sbuf_tensor("parts", [P, 17408], R32) as parts:
                pass
        W = sb("W", [P, SLOTS, 2048])
        tmp = sb("tmp", [P, TT, D])
        scr = sb("scr", [P, SCR])
        W_mod = sb("W_mod", [P, 2, 2048])
        x_tok = sb("x_tok", [P, TT, D])
        uT = sb("uT", [P, KC, S])
        y_tok = tmp
        gate_row = sb("gate_row", [P, D])
        gain_row = sb("gain_row", [P, D])
        att_0 = sb("att_0", [P, D])
        mod_bias = sb("mod_bias", [P, D])
        mod_out = sb("mod_out", [P, 256])
        cond = sb("cond", [P, JOBS, KC])
        cond_now = sb("cond_now", [P, KC, 32])
        cvec = sb("cvec_sb", [P, 2, 3, KC])
        shift_c = sb("shift_c", [P, KC])
        scale_c = sb("scale_c", [P, KC])
        stats = sb("stats", [P, 8, 6])
        mv = sb("mv", [P, 8, 2])
        rstd = sb("rstd", [P, 8])
        neg_max = sb("neg_max", [P, 2, 4])
        den = sb("den", [P, 16])
        key_max = sb("key_max", [P, 16])
        K = {n: sb("k_" + n, list(A[n].shape)) for n in CONSTS}
        qm = sb("qm", [P, 12, S])
        psum = ctx.enter_context(nc.psum_tensor("psum", [P, 8, 512], F32))

        def part(of, at, *shape):
            n = int(np.prod(shape))
            v = of[:, at:at + n]
            names = "abcd"[:len(shape)]
            if len(shape) > 1:
                v = v.rearrange(f"p ({' '.join(names)}) -> p {' '.join(names)}", **dict(zip(names[:-1], shape)))
            return v

        def carve(at, *shape):
            assert at + int(np.prod(shape)) <= SCR, (at, shape)
            return part(scr, at, *shape)

        silu_g = part(att_0, 0, 2, S)
        h_now = part(att_0, 512, 2, S)
        gu_hi = part(parts, 0, 2, 2, KC, P)
        gu_lo = part(parts, 4096, 2, 2, KC, P)
        d_hi = part(parts, 8192, 2, D)
        d_lo = part(parts, 10240, 2, D)
        u_hi = part(parts, 12288, KC, S)
        u_lo = part(parts, 14336, KC, S)
        h_hi = part(parts, 16384, 2, S)
        h_lo = part(parts, 16896, 2, S)
        proj = carve(0, TT, IN_W)
        kT = carve(6144, 6, S)
        att = [part(att_0, 0, 2, 3 * P), y_tok[:, :, 0:3 * P]]
        dil_pT = proj[:, :, 0:3 * P]
        stb_z = proj[:, :, DQ:DQ + 3 * P]
        stb_l = proj[:, :, SQ:SQ + 3 * P]
        rope_a, rope_b = tmp[:, 0, 0:512], tmp[:, 1, 0:512]
        proj2 = carve(0, TT, MIX2_W)
        ctx_kv = carve(2560, TT, 256)
        kT2 = carve(3072, 512)
        prob = carve(3584, 2, 512)
        probT = carve(4608, 2, 512)
        ctx_uT = carve(5632, KC, S)
        squares = carve(5632, TT, 12 * HD)
        pooledT = part(att_0, 0, 4, S)
        ctx_tok = tmp
        wm0, wm1 = W_mod[:, 0, :], W_mod[:, 1, :]
        pool_c = part(wm0, 0, 4, TT, S)
        bias_late = wm0[:, 0:D]
        w_grp = part(wm1, 0, 4, P)
        rope2 = part(wm1, 512, 2, TT, 32)
        qk_gain = part(wm1, 640, 2, HD)
        p_scale = wm1[:, 768:772]
        routeT = part(wm1, 800, 2, 32)
        slot_no = wm1[:, 880:1008]
        route = part(wm1, 1024, 4, S)
        w_router = part(mod_bias, 0, LAYERS, KC * EXPERTS)
        conv_w = part(mod_bias, 256, KC, 3)
        top8 = mod_bias[:, 300:308]
        conv_s = carve(0, 2, S + 2)
        conv_b = carve(600, 2, S)
        conv_c = carve(1200, 2, S)
        conv_z = carve(1800, 2, S)
        conv_yT = carve(3000, KC, S)
        xeT = carve(0, KC, EXPERTS * CAP)
        xe_now = carve(4096, KC, CAP)
        e_silu = carve(4352, S)
        e_h = carve(4608, S)
        e_hT = carve(4864, 2, P)
        R = carve(5120, D)
        G_now = carve(6144, TT, P)
        GT = carve(6400, S)
        sel = carve(6656, TT, EXPERTS * CAP)

        s_const = sem("constants_loaded")
        s_const2 = sem("constants2_loaded")
        s_x = sem("x_loaded")
        landed = [sem(f"landed{s}") for s in range(SLOTS)]
        mod_landed = [sem(f"mod_landed{s}") for s in range(2)]
        mod_freed = [sem(f"mod_freed{s}") for s in range(2)]
        bias_landed = sem("mod_bias_landed")
        zeroed = sem("zeroed")
        cond_sig = sem("cond_sigmoid")
        cond_made = sem("conditions")
        cond_set = sem("cond_now_set")
        bias_used = sem("mod_bias_used")
        mod_taken = sem("mod_taken")
        mod_stored = sem("mod_stored")
        hi_gu = sem("gate_up_high")
        hi_d = sem("down_high")
        lo_gu = sem("gate_up_low")
        lo_d = sem("down_low")
        u_low = sem("uT_low")
        pe_gu = sem("pe_gate_up")
        act_silu = sem("act_silu")
        dve_h = sem("dve_hidden")
        pe_down = sem("pe_down")
        cols_landed = sem("shift_scale_landed")
        cols_ready = sem("scale_plus_one")
        rows_landed = sem("gate_gain_landed")
        gated = sem("gate_applied")
        lnb_landed = sem("ln_bias_landed")
        lnb_late = sem("late_ln_bias_landed")
        pn_var = sem("norm_variance")
        pn_sqrt = sem("norm_sqrt")
        pn_x = sem("x_tok_tiles")
        tr_pe = sem("turned_banks")
        tr_act = sem("uT_half_act")
        tr_dve = sem("uT_half_dve")
        s_out = sem("out_stored")

        m_pe = steps("mixer_pe", [f"proj{n}" for n in range(12)] + [f"qk{g}" for g in range(6)] + ["A0", "A1"]
                     + sum([([f"B{b}"] if b < 4 else []) + [f"C{b}"] + ([f"A{b + 2}"] if b < 4 else [])
                            for b in range(6)], []) + ["out"])
        m_act = steps("mixer_act", [f"ev{n}" for n in range(12)] + ["silu_g", "qk0", "qk2", "qk4", "exp0", "ln1",
                                    "PT0", "exp2", "a1", "PT2", "ln3", "a3", "gn_sqrt"])
        m_dve = steps("mixer_dve", ["rot0", "rot1", "qk1", "qk3", "qk5", "max0", "na1", "p0", "lk1", "max2", "y0",
                                    "s1", "am1", "p2", "na3", "y1", "lk3", "y2", "s3", "r4", "am3", "r5", "y3",
                                    "gn_var", "y"])
        P2 = [f"c{t}" for t in range(TT)] + [f"p{t}{g}" for t in range(TT) for g in range(3)]
        m2_pe = steps("mix2_pe", P2 + ["pool0", "pool1", "grp0", "grp1", "kT", "q"] + ["S0", "S1", "T0", "S2"]
                      + sum([([f"T{n + 1}"] if n < 15 else []) + [f"V{n}"] + ([f"S{n + 3}"] if n < 13 else [])
                             for n in range(16)], [])
                      + ["yT0", "yT1", "out"])
        m2_act = steps("mix2_act", P2 + ["grp0", "grp1", "rms", "kT", "q"]
                       + ["e0"] + sum([([f"e{n + 1}"] if n < 15 else []) + [f"PT{n}"] for n in range(16)], []) + ["yT0"])
        m2_dve = steps("mix2_dve", ["pool0", "pool1", "sq", "rope", "q"] + [f"max{n}" for n in range(16)]
                       + ["y", "yT1"])
        cv_pe = steps("conv_pe", [f"f{fb}" for fb in range(KC)] + ["out"])
        cv_act = steps("conv_act", [f"f{fb}" for fb in range(KC)])
        cv_dve = steps("conv_dve", [f"f{fb}" for fb in range(KC)])
        r_pe = steps("router_pe", ["logits", "affT", "slotT"] + [f"g{k}" for k in range(KC)])
        r_act = steps("router_act", ["exp"] + [f"g{k}" for k in (0, 2, 4, 6)])
        r_dve = steps("router_dve", ["max", "aff", "slot", "sel"] + [f"g{k}" for k in (1, 3, 5, 7)])
        e_pe = steps("expert_pe", [f"k{k}" for k in range(KC)] + ["gT", "hT"] + [f"d{q}" for q in range(4)] + ["out"])
        e_act = steps("expert_act", ["silu", "hT", "R"])
        e_dve = steps("expert_dve", ["xG", "h", "gT", "R"])

        FFN_TILES = 2 * LAYERS * TILES
        MIXIN_S, MIXOUT_S = (6, 7, 0, 1, 2), (3, 4, 5, 8)

        fills = [2 * (2 * PAIRS + 1)] * 6 + [0] * MIX_SLOTS
        for s, c in zip(MIX_S, PER_LAYER):
            fills[s] = LAYERS * c
        before = {}
        for phase, slots_, units in (("in", MIXIN_S, 1), ("out", MIXOUT_S, 1), ("moe0", range(SLOTS), 2 * EXPERTS),
                                     ("cin", range(SLOTS), 1), ("cout", range(4), 1),
                                     ("moe1", range(SLOTS), 2 * EXPERTS)):
            for s in slots_:
                before[phase, s] = fills[s]
                fills[s] += units

        def slot_landed(phase, s, e=0):
            units = 2 * e + 2 if phase.startswith("moe") else 1
            return 16 * before[phase, s] + 16 * units

        block = ctx.enter_context(nc.Block())

        @block.sync
        def _(sp):
            sp.dma_start(x_tok[:, :, :], A["x"].rearrange("(t p) d -> p t d", p=P)).then_inc(s_x, 16)
            sp.wait_ge(zeroed, 1)

            def mod_chunk(job, c, first=None):
                if first is None or 2 * first + c // 2 > 0:
                    sp.wait_ge(mod_freed[c % 2], 2 * job + c // 2)
                if c == 0:
                    if first != 0:
                        sp.wait_ge(bias_used, job)
                    sp.dma_start(mod_bias[0:1, :], A["mod_b"][ds(job, 1), :]).then_inc(bias_landed, 16)
                src = A["mod_w"][ds(job, 1), 256 * c:256 * c + 256, :]
                sp.dma_start(part(W_mod[:, c % 2, :], 0, 2, D), src.rearrange("a (k p) n -> p (a k) n", p=P)
                             ).then_inc(mod_landed[c % 2], 16)

            for job in range(FIRST_JOBS):
                for c in range(4):
                    mod_chunk(job, c, job)
            sp.wait_ge(cols_landed, 32)

            def step_weights(l, k, parity, j, used, between=lambda: None):
                names = ("ffn1_w_gate", "ffn1_w_up", "ffn1_w_down") if k == 0 else ("ffn2_w_gate", "ffn2_w_up", "ffn2_w_down")
                b = 3 * ((parity + k) % 2)
                sp.wait_ge(lo_gu, used)
                for n in range(2):
                    src = A[names[n]][ds(l, 1), :, ds(j * STEP, STEP)]
                    sp.dma_start(part(W[:, b + n, :], 0, KC, STEP), src.rearrange("a (k p) n -> p (a k) n", p=P)
                                 ).then_inc(landed[b + n], 16)
                between()
                sp.wait_ge(lo_d, used)
                src = A[names[2]][ds(l, 1), ds(j * STEP, STEP), :]
                sp.dma_start(part(W[:, b + 2, :], 0, 2, D), src.rearrange("a (k p) n -> p (a k) n", p=P)
                             ).then_inc(landed[b + 2], 16)

            def ffn_stream(l, k):
                base = 1 + l * (2 * TILES) + k * TILES
                step_weights(l, k, 0, 0, base)
                with sp.Fori(0, PAIRS) as i:
                    for r in range(2):
                        def chunk(c):
                            mod_chunk(l * JOBS_LAYER + i + (FIRST_JOBS + 2 * PAIRS * k), c)
                        step_weights(l, k, r + 1, i * 2 + (r + 1), base + i * 4 + 2 * r, lambda: chunk(2 * r))
                        chunk(2 * r + 1)

            with sp.Fori(0, LAYERS) as l:
                ffn_stream(l, 0)
                for u in range(MIX_USES):
                    s = MIX_S[u % MIX_SLOTS]
                    if u >= MIX_SLOTS:
                        for c in (2 * (u % 2), 2 * (u % 2) + 1):
                            mod_chunk(l * JOBS_LAYER + (FIRST_JOBS + PAIRS + (u - MIX_SLOTS) // 2), c)
                    last = u - MIX_SLOTS
                    if u < 2:
                        sp.wait_ge(pn_x, l * 6 + 2)
                    elif u < 6:
                        sp.wait_ge(pe_down, l * (2 * TILES) + (1 + TILES))
                    else:
                        sp.wait_ge(m_pe.s, m_pe.at(f"proj{2 * (last // 2) + 1}", l))
                    if u < MIX_IN_USES:
                        g, half = u // 2, u % 2
                        src = A["w_in"][ds(l, 1), 512 * half:512 * half + 512, 512 * g:512 * g + 512]
                        dst = part(W[:, s, :], 0, 4, 512)
                    else:
                        r0 = 256 * (u - MIX_IN_USES)
                        src = A["w_out"][ds(l, 1), r0:r0 + 256, :]
                        dst = part(W[:, s, :], 0, 2, D)
                    sp.dma_start(dst, src.rearrange("a (k p) n -> p (a k) n", p=P)).then_inc(landed[s], 16)
                ffn_stream(l, 1)

            sp.wait_ge(m_pe.s, m_pe.at("out", LAYERS - 1))
            for g, s in enumerate(MIXIN_S):
                if g == 2:
                    sp.wait_ge(lo_gu, 1 + FFN_TILES)
                    sp.wait_ge(lo_d, 1 + FFN_TILES)
                sp.dma_start(part(W[:, s, :], 0, KC, 256),
                             A["w_mix_in"][:, 256 * g:256 * g + 256].rearrange("(k p) n -> p k n", p=P)
                             ).then_inc(landed[s], 16)

            def rows_of(w, s, g):
                sp.dma_start(part(W[:, s, :], 0, 2, D), w[256 * g:256 * g + 256, :].rearrange("(k p) n -> p k n", p=P)
                             ).then_inc(landed[s], 16)

            for g in range(4):
                if g == 3:
                    sp.wait_ge(pe_down, 1 + FFN_TILES)
                rows_of(A["w_mix_out"], MIXOUT_S[g], g)

            def expert_slot(layer, e, s):
                if s < KC:
                    for n, w in enumerate((A["w_exp_gate"], A["w_exp_up"])):
                        sp.dma_start(W[:, s, D * n:D * n + D], w[layer, ds(e, 1), P * s:P * s + P, :]
                                     .rearrange("a p n -> p (a n)")).then_inc(landed[s], 16)
                else:
                    r0 = 256 * (s - KC)
                    sp.dma_start(part(W[:, s, :], 0, 2, D), A["w_exp_down"][layer, ds(e, 1), r0:r0 + 256, :]
                                 .rearrange("a (k p) n -> p (a k) n", p=P)).then_inc(landed[s], 32)

            def slot_use(s):
                return f"k{s}" if s < KC else f"d{s - KC}"

            def expert_stream(layer, first_wait):
                for s in first_wait:
                    sem_, n = first_wait[s]
                    sp.wait_ge(sem_, n)
                    expert_slot(layer, 0, s)
                with sp.Fori(1, EXPERTS) as e:
                    for s in range(SLOTS):
                        sp.wait_ge(e_pe.s, e_pe.at(slot_use(s), e + (EXPERTS * layer - 1)))
                        expert_slot(layer, e, s)

            free = {s: (pe_down, 1 + FFN_TILES) for s in (9, 10, 11)}
            free |= {s: (m2_pe.s, m2_pe.at("p12")) for s in MIXIN_S}
            free |= {s: (m2_pe.s, m2_pe.at("out")) for s in MIXOUT_S}
            expert_stream(0, dict(sorted(free.items(), key=lambda f: f[1][1] if f[1][0] is m2_pe.s else -1)))
            for u in range(12):
                sp.wait_ge(e_pe.s, e_pe.at(slot_use(u), EXPERTS - 1))
                c0 = D * (u % 3) + 256 * (u // 3)
                sp.dma_start(part(W[:, u, :], 0, KC, 256), A["w_conv_in"][:, c0:c0 + 256]
                             .rearrange("(k p) n -> p k n", p=P)).then_inc(landed[u], 16)
            for s in range(4):
                sp.wait_ge(cv_pe.s, cv_pe.at(f"f{2 * (s // 3) + 1}"))
                rows_of(A["w_conv_out"], s, s)
            free = {s: (cv_pe.s, cv_pe.at(f"f{2 * (s // 3) + 1}")) for s in range(4, SLOTS)}
            free |= {s: (cv_pe.s, cv_pe.at("out")) for s in range(4)}
            expert_stream(1, free)
            for t in range(TT):
                sp.wait_ge(pn_x, 2 + 2 * 9 + t + 1)
                sp.dma_start(out[P * t:P * t + P, :], x_tok[:, t, :]).then_inc(s_out, 16)
            sp.wait_ge(s_out, 16 * TT)

        @block.gpsimd
        def _(pool):
            pool.memset(mod_bias[:, :], 0.0).then_inc(zeroed, 1)
            pool.dma_start(cvec[:, 0, :, :], A["cvec"]).then_inc(s_const, 16)
            for name in CONSTS:
                pool.dma_start(K[name][:], A[name]).then_inc(s_const, 16)
            pool.memset(qm[:, 0:6, :], 0.0).then_inc(zeroed, 1)
            pool.memset(qm[:, 6:12, :], 0.0).then_inc(zeroed, 1)

            def columns(row, need=None):
                if need is not None:
                    pool.wait_ge(mod_stored, need)
                    pool.wait_ge(zeroed, 3)
                for n, dst in enumerate((shift_c, scale_c)):
                    pool.dma_start(dst[:, :], mod_rows[ds(row + n, 1), :].rearrange("a (k p) -> p (a k)", p=P)
                                   ).then_inc(cols_landed, 16)

            def rows(p, row, need=None):
                if need is not None:
                    pool.wait_ge(mod_stored, need)
                pool.wait_ge(pn_x, p * 2 + 2)
                pool.wait_ge(zeroed, 3)
                pool.dma_start(gate_row[:, :], mod_rows[ds(row, 1), :].to_broadcast([P, D])).then_inc(rows_landed, 16)
                pool.dma_start(gain_row[:, :], A["ln_g"][ds(p, 1), :].to_broadcast([P, D])).then_inc(rows_landed, 16)

            def set_cond(job, first=False):
                if not first:
                    pool.wait_ge(mod_freed[1], job * 2)
                pool.tensor_copy(cond_now[:, :, :], cond[:, ds(job, 1), :].rearrange("p a k -> p (a k)").unsqueeze(2)
                                 .to_broadcast([P, KC, 32])).then_inc(cond_set, 1)

            pool.wait_ge(cond_made, 1)
            for job in range(FIRST_JOBS):
                set_cond(job, job == 0)
            with pool.Fori(0, LAYERS) as l:
                for k in range(3):
                    turned = l * 4 + (1 + (k if k < 2 else 3))
                    pool.wait_ge(tr_act, turned)
                    pool.wait_ge(tr_dve, turned)
                    columns(l * 9 + 3 * k, l * (9 * 16) + 16 * (3 * k + 2))
                    if k in (0, 2):
                        with pool.Fori(0, PAIRS) as j:
                            set_cond(l * JOBS_LAYER + j + (FIRST_JOBS + PAIRS * k))
                    rows(l * 3 + k, l * 9 + (3 * k + 2), l * (9 * 16) + 16 * (3 * k + 3))
                    if k == 1:
                        with pool.Fori(0, PAIRS) as j:
                            set_cond(l * JOBS_LAYER + j + (FIRST_JOBS + PAIRS))
            for c, (p, turned) in enumerate(((6, 9), (7, 11), (8, 12), (9, 13))):
                row = MOD2 + 3 * c
                pool.wait_ge(tr_act, turned)
                pool.wait_ge(tr_dve, turned)
                if c == 2:
                    pool.wait_ge(r_act.s, r_act.at("g6"))
                    pool.wait_ge(r_dve.s, r_dve.at("g7"))
                columns(row, 16 * JOBS if c == 0 else None)
                rows(p, row + 2)
                if p > 6:
                    pool.dma_start(bias_late, A["ln_b"][p:p + 1, :].to_broadcast([P, D])).then_inc(lnb_late, 16)
                if c == 0:
                    for n in CONSTS2:
                        dst = {"pool": pool_c, "w_grp": w_grp, "rope2": rope2, "qk_gain": qk_gain, "p_scale": p_scale,
                               "w_router": w_router, "conv_w": conv_w, "slot_no": slot_no}[n]
                        pool.dma_start(dst, A[n]).then_inc(s_const2, 16)
                    pool.dma_start(ctx_tok[:, :, :], A["ctx"].rearrange("(t p) d -> p t d", p=P)).then_inc(s_const2, 16)
                    pool.wait_ge(tr_act, 10)
                    pool.wait_ge(tr_dve, 10)
                    columns(CTX_ROW)

        @block.tensor
        def _(pe):
            pe.wait_ge(s_const, 16 * (len(CONSTS) + 1))
            ident = K["ident"]

            def mod_quarter(job, c, bank=6, first=False):
                if c == 0:
                    pe.wait_ge(bias_landed, job * 16 + 16)
                    if not first:
                        pe.wait_ge(mod_taken, job)
                    for q in range(4):
                        ins = pe.matmul(psum[32 * q:32 * q + 32, bank, 0:256], K["ones"][:, 0:32], mod_bias[:, 256 * q:256 * q + 256],
                                        start=True, stop=False, skip_group_check=True)
                    ins.then_inc(bias_used, 1)
                    pe.wait_ge(cond_set, job + 1)
                pe.wait_ge(mod_landed[c % 2], job * 32 + 16 * (c // 2 + 1))
                for kk in range(2):
                    for q in range(4):
                        ins = pe.matmul(psum[32 * q:32 * q + 32, bank, 0:256], cond_now[:, 2 * c + kk, :],
                                        part(W_mod[:, c % 2, :], 0, 2, D)[:, kk, 256 * q:256 * q + 256],
                                        start=False, stop=(c == 3 and kk == 1), skip_group_check=True)
                ins.then_inc(mod_freed[c % 2], 1)

            def turn(src, ready):
                for b in range(4):
                    for q in range(2):
                        for t in range(TT):
                            if b == 0 and q == 0:
                                pe.wait_ge(*ready(t))
                            c = P * (2 * b + q)
                            ins = pe.transpose(psum[:, 4 + b, S * q + P * t:S * q + P * t + P], src[:, t, c:c + P], ident[:, :])
                    ins.then_inc(tr_pe, 1)

            def turned(inst):
                pe.wait_ge(tr_act, inst + 2)
                pe.wait_ge(tr_dve, inst + 2)

            def ffn(l, k):
                f0 = 1 + l * (2 * TILES) + k * TILES
                def gate_up(t, i=0):
                    pe.wait_ge(lo_gu, f0 + i * 4 + (t + 1))
                    if t >= 2:
                        pe.wait_ge(dve_h, f0 + i * 4 + (t - 1))
                    for g in range(2):
                        for n, (w, u) in enumerate(((gu_hi, u_hi), (gu_lo, u_hi), (gu_hi, u_lo))):
                            if t == 0 and g == 0 and n == 2:
                                pe.wait_ge(u_low, l * 2 + (k + 1))
                            for kc in range(KC):
                                ins = pe.matmul(psum[:, 4 + t % 2, S * g:S * g + S], w[:, t % 2, g, kc, :],
                                                u[:, kc, :], start=(n == 0 and kc == 0),
                                                stop=(n == 2 and kc == KC - 1))
                    ins.then_inc(pe_gu, 1)

                def down(t, i=0):
                    pe.wait_ge(lo_d, f0 + i * 4 + (t + 1))
                    pe.wait_ge(dve_h, f0 + i * 4 + (t + 1))
                    for tt in range(TT):
                        for n, (h_, w) in enumerate(((h_hi, d_hi), (h_hi, d_lo), (h_lo, d_hi))):
                            for h in range(2):
                                ins = pe.matmul(psum[:, 2 * tt + h, :], h_[:, t % 2, P * tt:P * tt + P],
                                                w[:, t % 2, 512 * h:512 * h + 512], start=(t == 0 and n == 0),
                                                stop=(t == TILES - 1 and n == 2), skip_group_check=True)
                    ins.then_inc(pe_down, 1)

                gate_up(0)
                gate_up(1)
                down(0)
                with pe.Fori(0, PAIRS) as i:
                    for t in range(1, 5):
                        gate_up(t + 1, i)
                        if t % 2:
                            for c in (t - 1, t):
                                mod_quarter(l * JOBS_LAYER + i + (FIRST_JOBS + 2 * PAIRS * k), c)
                        down(t, i)
                down(TILES - 1)
                pe.wait_ge(mod_taken, l * JOBS_LAYER + (FIRST_JOBS + PAIRS + 2 * PAIRS * k))

            def times_rows(src, slots):
                for u in range(4):
                    w = part(W[:, slots(u), :], 0, 2, D)
                    for kk in range(2):
                        kc = 2 * u + kk
                        for tt in range(TT):
                            for h in range(2):
                                ins = pe.matmul(psum[:, 2 * tt + h, :], src[:, kc, P * tt:P * tt + P],
                                                w[:, kk, 512 * h:512 * h + 512], start=(kc == 0), stop=(kc == KC - 1),
                                                skip_group_check=True)
                return ins

            def mixer(l):
                def slot(u):
                    s = u % MIX_SLOTS
                    pe.wait_ge(landed[MIX_S[s]], (l * PER_LAYER[s] + (u // MIX_SLOTS + 1)) * 16)
                    return MIX_S[s]

                for g in range(6):
                    for t in range(TT):
                        n = 2 * g + t
                        if n >= 4:
                            pe.wait_ge(m_act.s, m_act.at(f"ev{n - 4}", l))
                        for kc in range(KC):
                            u = 2 * g + kc // 4
                            s = slot(u) if kc % 4 == 0 else MIX_S[u % MIX_SLOTS]
                            ins = pe.matmul(psum[:, 4 + n % 4, :], uT[:, kc, P * t:P * t + P],
                                            part(W[:, s, :], 0, 4, 512)[:, kc % 4, :], start=(kc == 0), stop=(kc == KC - 1))
                            if kc == 3 and g:
                                mod_quarter(l * JOBS_LAYER + (FIRST_JOBS + PAIRS + g - 1), 2 * t, bank=0)
                        ins.then_inc(m_pe.sig(f"proj{n}"), 1)
                        if g:
                            mod_quarter(l * JOBS_LAYER + (FIRST_JOBS + PAIRS + g - 1), 2 * t + 1, bank=0)
                pe.wait_ge(mod_taken, l * JOBS_LAYER + (FIRST_JOBS + 2 * PAIRS))
                for g in range(6):
                    kind, hb = g // 2, g % 2
                    if g < 4:
                        pe.wait_ge(m_act.s, m_act.at(f"ev{8 + g}", l))
                    if g == 0:
                        pe.wait_ge(m_dve.s, m_dve.at("rot0", l))
                    if g == 2:
                        pe.wait_ge(m_dve.s, m_dve.at("rot1", l))
                    if g == 4:
                        pe.wait_ge(m_act.s, m_act.at("qk0", l))
                        pe.wait_ge(m_act.s, m_act.at("ev11", l))
                    if g == 5:
                        pe.wait_ge(m_dve.s, m_dve.at("qk1", l))
                    for n, col in enumerate((QCOL[kind], KCOL[kind])):
                        for t in range(TT):
                            ins = pe.transpose(psum[:, 4 + g % 4, S * n + P * t:S * n + P * t + P],
                                               proj[:, t, col + P * hb:col + P * hb + P], ident[:, :])
                    ins.then_inc(m_pe.sig(f"qk{g}"), 1)

                def scores(b):
                    kind, hb = ATT[b]
                    for hh in range(2):
                        q, k_ = qm[:, NH * kind + 2 * hb + hh, :], kT[:, 2 * kind + hb, :]
                        bk = psum[:, 4 + 2 * (b % 2) + hh, :]
                        if kind == DIL:
                            pe.matmul(bk[:, 0:P], q[:, 0:P], k_[:, 0:P], start=True, stop=True)
                            ins = pe.matmul(bk[:, P:3 * P], q[:, P:S], k_[:, :], start=True, stop=True)
                        else:
                            pe.matmul(bk[:, 0:S], k_[:, 0:P], q[:, :], start=True, stop=True)
                            ins = pe.matmul(bk[:, S:3 * P], k_[:, P:S], q[:, P:S], start=True, stop=True)
                    ins.then_inc(m_pe.sig(f"A{b}"), 1)

                def second(b):
                    kind, hb = ATT[b]
                    bk = psum[:, 4 + 2 * (b % 2):6 + 2 * (b % 2), :]
                    if kind == DIL:
                        pe.wait_ge(m_dve.s, m_dve.at(f"p{b}", l))
                        for hh in range(2):
                            for c in range(3):
                                ins = pe.transpose(bk[:, hh, P * c:P * c + P], att[b % 2][:, hh, P * c:P * c + P], ident[:, :])
                    else:
                        pe.wait_ge(m_dve.s, m_dve.at(f"lk{b}", l))
                        for hh in range(2):
                            lk = stb_z[:, hh, :]
                            pe.matmul(bk[:, hh, 0:3 * P], K["later"][:, :], lk, start=True, stop=False, skip_group_check=True)
                            ins = pe.matmul(bk[:, hh, P:S], K["ones"][:, :], lk[:, S:3 * P], start=False, stop=True,
                                            skip_group_check=True)
                    ins.then_inc(m_pe.sig(f"B{b}"), 1)

                def values(b):
                    kind, hb = ATT[b]
                    if kind == DIL:
                        pe.wait_ge(m_act.s, m_act.at(f"PT{b}", l))
                    elif kind == STB:
                        pe.wait_ge(m_dve.s, m_dve.at(f"am{b}", l))
                    else:
                        pe.wait_ge(m_dve.s, m_dve.at(f"r{b}", l))
                    for hh in range(2):
                        h, w = 2 * hb + hh, VW[kind]
                        pT = dil_pT[:, hh, :] if kind == DIL else att[b % 2][:, hh, :]
                        v = proj[:, :, VCOL[kind] + w * h:VCOL[kind] + w * h + w]
                        if kind == RET:
                            o = [psum[:, t, w * h:w * h + w] for t in range(TT)]
                        else:
                            o = [psum[:, 1 + kind, S * t + w * h:S * t + w * h + w] for t in range(TT)]
                        pe.matmul(o[0], pT[:, 0:P], v[:, 0, :], start=True, stop=True)
                        pe.matmul(o[1], pT[:, P:S], v[:, 0, :], start=True, stop=False)
                        ins = pe.matmul(o[1], pT[:, S:3 * P], v[:, 1, :], start=False, stop=True)
                    ins.then_inc(m_pe.sig(f"C{b}"), 1)

                for g in (2, 4):
                    pe.wait_ge(m_act.s, m_act.at(f"qk{g}", l))
                pe.wait_ge(m_dve.s, m_dve.at("qk5", l))
                scores(0)
                scores(1)
                for b in range(6):
                    if b < 4:
                        second(b)
                    if b == 2:
                        pe.wait_ge(m_dve.s, m_dve.at("y0", l))
                    if b == 3:
                        pe.wait_ge(m_dve.s, m_dve.at("y1", l))
                    values(b)
                    if b < 4:
                        if ATT[b][0] == STB:
                            pe.wait_ge(m_dve.s, m_dve.at(f"s{b}", l))
                        scores(b + 2)
                turn(y_tok, lambda t: (m_dve.s, m_dve.at("y", l)))
                turned(l * 4 + 2)
                times_rows(uT, lambda u: slot(MIX_IN_USES + u)).then_inc(m_pe.sig("out"), 1)

            for job in range(FIRST_JOBS):
                for c in range(4):
                    mod_quarter(job, c, first=job == 0)
            pe.wait_ge(mod_taken, FIRST_JOBS)
            with pe.Fori(0, LAYERS) as l:
                turn(x_tok, lambda t: (pn_x, l * 6 + (t + 1)))
                turned(l * 4)
                ffn(l, 0)
                turn(x_tok, lambda t: (pn_x, l * 6 + (t + 3)))
                turned(l * 4 + 1)
                mixer(l)
                turn(x_tok, lambda t: (pn_x, l * 6 + (t + 5)))
                turned(l * 4 + 3)
                ffn(l, 1)

            turn(x_tok, lambda t: (pn_x, 12 + t + 1))
            turned(8)
            turn(ctx_tok, lambda t: (s_const2, 16 * (len(CONSTS2) + 1)))
            turned(9)

            def in_slot(phase, s):
                pe.wait_ge(landed[s], slot_landed(phase, s))
                return s
            for t in range(TT):
                s = in_slot("in", MIXIN_S[2]) if t == 0 else MIXIN_S[2]
                for kc in range(KC):
                    ins = pe.matmul(psum[:, 6 + t, 0:256], ctx_uT[:, kc, P * t:P * t + P], part(W[:, s, :], 0, KC, 256)[:, kc, :],
                                    start=(kc == 0), stop=(kc == KC - 1))
                ins.then_inc(m2_pe.sig(f"c{t}"), 1)
            for t in range(TT):
                for b in range(3):
                    for g in (2 * b, 2 * b + 1)[:1 if b == 2 else 2]:
                        s = in_slot("in", MIXIN_S[g]) if t == 0 else MIXIN_S[g]
                        for kc in range(KC):
                            ins = pe.matmul(psum[:, 3 * t + b, 256 * (g % 2):256 * (g % 2) + 256], uT[:, kc, P * t:P * t + P],
                                            part(W[:, s, :], 0, KC, 256)[:, kc, :], start=(kc == 0), stop=(kc == KC - 1))
                    ins.then_inc(m2_pe.sig(f"p{t}{b}"), 1)
            pe.wait_ge(m2_act.s, m2_act.at("p12"))
            for i in range(2):
                for g in (2 * i, 2 * i + 1):
                    for t in range(TT):
                        ins = pe.matmul(psum[:, 2 + i, S * (g % 2):S * (g % 2) + S], proj2[:, t, 768 + P * g:768 + P * g + P],
                                        pool_c[:, g, t, :], start=(t == 0), stop=(t == TT - 1))
                ins.then_inc(m2_pe.sig(f"pool{i}"), 1)
            for i in range(2):
                pe.wait_ge(m2_dve.s, m2_dve.at(f"pool{i}"))
                for g in (2 * i, 2 * i + 1):
                    ins = pe.matmul(psum[:, 2 + i, S * (g % 2):S * (g % 2) + S], w_grp[:, g, :], pooledT[:, g, :],
                                    start=True, stop=True)
                ins.then_inc(m2_pe.sig(f"grp{i}"), 1)
            pe.wait_ge(m2_dve.s, m2_dve.at("rope"))
            for n, src in enumerate((ctx_kv[:, 0, 0:P], ctx_kv[:, 1, 0:P], proj2[:, 0, 512:640], proj2[:, 1, 512:640])):
                ins = pe.transpose(psum[:, 4, P * n:P * n + P], src, ident[:, :])
            ins.then_inc(m2_pe.sig("kT"), 1)
            for j in range(4):
                for t in range(TT):
                    c = S * (j % 2) + P * t
                    ins = pe.transpose(psum[:, 5 + j // 2, c:c + P], proj2[:, t, P * j:P * j + P], ident[:, :])
            ins.then_inc(m2_pe.sig("q"), 1)
            pe.wait_ge(m2_act.s, m2_act.at("q"))
            pe.wait_ge(m2_dve.s, m2_dve.at("q"))

            def qk2(n):
                h, t = n // 2, n % 2
                pe.matmul(psum[:, 4 + n % 2, :], qm[:, 2 * (h % 4) + h // 4, P * t:P * t + P], kT2[:, :],
                          start=True, stop=True).then_inc(m2_pe.sig(f"S{n}"), 1)
            def prob_turned(n):
                pe.wait_ge(m2_act.s, m2_act.at(f"e{n}"))
                for c in range(4):
                    ins = pe.transpose(psum[:, 6 + n % 2, P * c:P * c + P], prob[:, n % 2, P * c:P * c + P], ident[:, :])
                ins.then_inc(m2_pe.sig(f"T{n}"), 1)
            qk2(0)
            qk2(1)
            prob_turned(0)
            qk2(2)
            for n in range(16):
                h, t = n // 2, n % 2
                if n < 15:
                    prob_turned(n + 1)
                pe.wait_ge(m2_act.s, m2_act.at(f"PT{n}"))
                kv = 128 + HD * (h // 4)
                for c, v in enumerate((ctx_kv[:, 0, kv:kv + HD], ctx_kv[:, 1, kv:kv + HD],
                                       proj2[:, 0, 512 + kv:512 + kv + HD], proj2[:, 1, 512 + kv:512 + kv + HD])):
                    ins = pe.matmul(psum[:, t, HD * h:HD * h + HD], probT[:, n % 2, P * c:P * c + P], v,
                                    start=(c == 0), stop=(c == 3))
                ins.then_inc(m2_pe.sig(f"V{n}"), 1)
                if n < 13:
                    qk2(n + 3)
            pe.wait_ge(m2_dve.s, m2_dve.at("y"))
            for b in range(2):
                for q in range(2):
                    for t in range(TT):
                        c = P * (2 * b + q)
                        ins = pe.transpose(psum[:, 4 + b, S * q + P * t:S * q + P * t + P], proj2[:, t, c:c + P], ident[:, :])
                ins.then_inc(m2_pe.sig(f"yT{b}"), 1)
            pe.wait_ge(m2_act.s, m2_act.at("yT0"))
            pe.wait_ge(m2_dve.s, m2_dve.at("yT1"))
            times_rows(uT, lambda u: in_slot("out", MIXOUT_S[u])).then_inc(m2_pe.sig("out"), 1)

            def experts(layer):
                for t in range(TT):
                    for kc in range(KC):
                        ins = pe.matmul(psum[:, 4, EXPERTS * t:EXPERTS * t + EXPERTS], uT[:, kc, P * t:P * t + P],
                                        part(w_router[:, layer, :], 0, KC, EXPERTS)[:, kc, :], start=(kc == 0), stop=(kc == KC - 1))
                ins.then_inc(r_pe.sig("logits"), 1)
                pe.wait_ge(r_dve.s, r_dve.at("aff", layer))
                for t in range(TT):
                    ins = pe.transpose(psum[0:EXPERTS, 5, P * t:P * t + P], routeT[:, t, EXPERTS:2 * EXPERTS], ident[:, :])
                ins.then_inc(r_pe.sig("affT"), 1)
                pe.wait_ge(r_dve.s, r_dve.at("slot", layer))
                for t in range(TT):
                    ins = pe.transpose(psum[:, 5, EXPERTS * t:EXPERTS * t + EXPERTS], route[0:EXPERTS, 3, P * t:P * t + P],
                                       ident[0:EXPERTS, 0:EXPERTS])
                ins.then_inc(r_pe.sig("slotT"), 1)
                pe.wait_ge(r_dve.s, r_dve.at("sel", layer))
                for kc in range(KC):
                    for t in range(TT):
                        ins = pe.matmul(psum[:, kc, :], x_tok[:, t, P * kc:P * kc + P], sel[:, t, :],
                                        start=(t == 0), stop=(t == TT - 1))
                    ins.then_inc(r_pe.sig(f"g{kc}"), 1)
                pe.wait_ge(r_act.s, r_act.at("g6", layer))
                pe.wait_ge(r_dve.s, r_dve.at("g7", layer))

                def expert(e, first):
                    E = e + EXPERTS * layer
                    pe.wait_ge(e_dve.s, e_dve.at("xG", E))
                    for kc in range(KC):
                        pe.wait_ge(landed[kc], e * 32 + slot_landed(f"moe{layer}", kc))
                        w = part(W[:, kc, :], 0, 2, 4, 256)
                        for q in range(4):
                            ins = pe.matmul(psum[32 * q:32 * q + 32, 4, :].rearrange("p (g n) -> p g n", g=2),
                                            xe_now[:, kc, :], w[:, :, q, :], start=(kc == 0), stop=(kc == KC - 1),
                                            skip_group_check=True)
                        ins.then_inc(e_pe.sig(f"k{kc}"), 1)
                    for t in range(TT):
                        ins = pe.transpose(psum[:, 7, P * t:P * t + P], G_now[:, t, :], ident[:, :])
                    ins.then_inc(e_pe.sig("gT"), 1)
                    pe.wait_ge(e_dve.s, e_dve.at("h", E))
                    for j in range(2):
                        ins = pe.transpose(psum[:, 5, P * j:P * j + P], e_h[:, P * j:P * j + P], ident[:, :])
                    ins.then_inc(e_pe.sig("hT"), 1)
                    pe.wait_ge(e_act.s, e_act.at("hT", E))
                    for c in range(KC):
                        s = KC + c // 2
                        if c % 2 == 0:
                            pe.wait_ge(landed[s], e * 32 + slot_landed(f"moe{layer}", s))
                        for q in range(4):
                            ins = pe.matmul(psum[32 * q:32 * q + 32, 6, 0:256], e_hT[:, c % 2, 32 * (c // 2):32 * (c // 2) + 32],
                                            part(W[:, s, :], 0, 2, D)[:, c % 2, 256 * q:256 * q + 256],
                                            start=(c == 0), stop=(c == KC - 1), skip_group_check=True)
                        if c % 2:
                            ins.then_inc(e_pe.sig(f"d{c // 2}"), 1)
                    pe.wait_ge(e_act.s, e_act.at("R", E))
                    pe.wait_ge(e_dve.s, e_dve.at("R", E))
                    for tt in range(TT):
                        for h in range(2):
                            ins = pe.matmul(psum[:, 2 * tt + h, :], GT[:, P * tt:P * tt + P], R[:, 512 * h:512 * h + 512],
                                            start=first, stop=True, skip_group_check=True)
                    ins.then_inc(e_pe.sig("out"), 1)

                expert(0, True)
                with pe.Fori(1, EXPERTS) as e:
                    expert(e, False)

            turn(x_tok, lambda t: (pn_x, 14 + t + 1))
            turned(10)
            experts(0)

            turn(x_tok, lambda t: (pn_x, 16 + t + 1))
            turned(11)
            for fb in range(KC):
                if fb >= 2:
                    pe.wait_ge(cv_dve.s, cv_dve.at(f"f{fb - 2}"))
                for n in range(3):
                    s = 3 * (fb // 2) + n
                    if fb % 2 == 0:
                        in_slot("cin", s)
                    o = psum[:, 4 + 2 * (fb % 2) + n // 2, S * (n % 2):S * (n % 2) + S]
                    for kc in range(KC):
                        ins = pe.matmul(o, part(W[:, s, :], 0, KC, 256)[:, kc, P * (fb % 2):P * (fb % 2) + P], uT[:, kc, :],
                                        start=(kc == 0), stop=(kc == KC - 1))
                ins.then_inc(cv_pe.sig(f"f{fb}"), 1)
            pe.wait_ge(cv_dve.s, cv_dve.at("f7"))
            times_rows(conv_yT, lambda u: in_slot("cout", u)).then_inc(cv_pe.sig("out"), 1)
            turn(x_tok, lambda t: (pn_x, 18 + t + 1))
            turned(12)
            experts(1)

        @block.scalar
        def _(act):
            copy = ACT.Identity

            def mod_row(job, first=False, bank=6):
                act.wait_ge(mod_freed[1], job * 2 + 2)
                if not first:
                    act.wait_ge(mod_stored, job * 16)
                act.activation(mod_out[:, :], psum[:, bank, 0:256], copy).then_inc(mod_taken, 1)
                act.wait_ge(mod_taken, job + 1)
                act.dma_start(mod_rows[ds(job, 1), :].rearrange("a (h n) -> (a h) n", h=4), mod_out[0:97:32, :]
                              ).then_inc(mod_stored, 16)

            def turn(inst, m, dst=uT, split=False):
                if m is not None:
                    act.wait_ge(cols_ready, m + 1)
                for b in range(2):
                    act.wait_ge(tr_pe, inst * 4 + (b + 1))
                    for q in range(2):
                        kc = 2 * b + q
                        src = psum[:, 4 + b, S * q:S * q + S]
                        if m is None:
                            ins = act.activation(dst[:, kc, :], src, copy)
                        else:
                            for o in (dst[:, kc, :], u_hi[:, kc, :])[:1 + split]:
                                ins = act.activation(o, src, copy, bias=shift_c[:, kc:kc + 1], scale=scale_c[:, kc:kc + 1])
                ins.then_inc(tr_act, 1)

            def norm(p, late=False):
                if not late:
                    act.wait_ge(gated, p + 1)
                    act.dma_start(gate_row[:, :], A["ln_b"][ds(p, 1), :].to_broadcast([P, D])).then_inc(lnb_landed, 16)
                act.wait_ge(pn_var, p + 1)
                act.activation(rstd[:, 0:TT], rstd[:, 0:TT], ACT.Sqrt).then_inc(pn_sqrt, 1)

            def ffn(l, k):
                f0 = 1 + l * (2 * TILES) + k * TILES
                fill0 = [l * (2 * PAIRS + 1) + (0, PAIRS + 1 - q)[k] for q in range(2)]

                def slots_of(t, i=0):
                    q = (t // 2 + k) % 2
                    return 3 * q, (fill0[q] + i + (t // 4 + 1)) * 16

                def high_gate_up(t, i=0):
                    b, n = slots_of(t, i)
                    if t % 2 == 0:
                        act.wait_ge(landed[b], n)
                        act.wait_ge(landed[b + 1], n)
                    act.wait_ge(pe_gu, f0 + i * 4 + (t - 1) if t else f0)
                    for g in range(2):
                        ins = act.activation(gu_hi[:, t % 2, g, :, :],
                                             part(W[:, b + g, :], 0, KC, STEP)[:, :, P * (t % 2):P * (t % 2) + P], copy)
                    ins.then_inc(hi_gu, 1)

                def high_down(t, i=0):
                    b, n = slots_of(t, i)
                    if t % 2 == 0:
                        act.wait_ge(landed[b + 2], n)
                    act.wait_ge(pe_down, f0 + i * 4 + (t - 1) if t else f0)
                    act.activation(d_hi[:, t % 2, :], part(W[:, b + 2, :], 0, 2, D)[:, t % 2, :], copy
                                   ).then_inc(hi_d, 1)

                def silu(t, i=0):
                    act.wait_ge(pe_gu, f0 + i * 4 + (t + 1))
                    if t >= 1:
                        act.wait_ge(dve_h, f0 + i * 4 + (t - 1))
                    act.activation(silu_g[:, t % 2, :], psum[:, 4 + t % 2, 0:S], ACT.Silu).then_inc(act_silu, 1)
                high_gate_up(0)
                high_gate_up(1)
                turn(l * 4 + (0, 3)[k], l * 3 + 2 * k, split=True)
                high_down(0)
                silu(0)
                with act.Fori(0, PAIRS) as i:
                    for t in range(1, 5):
                        high_gate_up(t + 1, i)
                        high_down(t, i)
                        silu(t, i)
                        if t == 4:
                            mod_row(l * JOBS_LAYER + i + (FIRST_JOBS + 2 * PAIRS * k))
                high_down(TILES - 1)
                silu(TILES - 1)

            def mixer(l):
                for n in range(12):
                    act.wait_ge(m_pe.s, m_pe.at(f"proj{n}", l))
                    act.activation(proj[:, n % 2, 512 * (n // 2):512 * (n // 2) + 512], psum[:, 4 + n % 4, :], copy
                                   ).then_inc(m_act.sig(f"ev{n}"), 1)
                    if n % 2 and n > 1:
                        mod_row(l * JOBS_LAYER + (FIRST_JOBS + PAIRS + n // 2 - 1), bank=0)
                act.drain()
                act.activation(proj[:, :, RG:RG + 512], proj[:, :, RG:RG + 512], ACT.Silu).then_inc(m_act.sig("silu_g"), 1)
                for g in (0, 2, 4):
                    kind, hb = g // 2, g % 2
                    bk = psum[:, 4 + g % 4, :]
                    act.wait_ge(m_pe.s, m_pe.at(f"qk{g}", l))
                    for hh in range(2):
                        rows_ = slice(64 * hh, 64 * hh + 64)
                        act.activation(qm[rows_, NH * kind + 2 * hb + hh, :], bk[rows_, 0:S], copy)
                    act.activation(kT[:, 2 * kind + hb, :], bk[:, S:2 * S], copy).then_inc(m_act.sig(f"qk{g}"), 1)

                def exps(b):
                    act.wait_ge(m_dve.s, m_dve.at(f"max{b}", l))
                    for hh in range(2):
                        for t in range(TT):
                            blk = att[b % 2][:, hh, 0:P] if t == 0 else att[b % 2][:, hh, P:3 * P]
                            ins = act.activation(blk, blk, ACT.Exp, bias=neg_max[:, b // 2, 2 * hh + t:2 * hh + t + 1])
                    ins.then_inc(m_act.sig(f"exp{b}"), 1)

                def logs(b):
                    act.wait_ge(m_dve.s, m_dve.at(f"na{b}", l))
                    act.activation(stb_l, stb_l, ACT.Exp)
                    act.drain()
                    act.activation(stb_l, stb_l, ACT.Ln, bias=K["ones"][:, 0:1]).then_inc(m_act.sig(f"ln{b}"), 1)

                def p_turned(b):
                    act.wait_ge(m_pe.s, m_pe.at(f"B{b}", l))
                    act.activation(dil_pT, psum[:, 4 + 2 * (b % 2):6 + 2 * (b % 2), 0:3 * P], copy
                                   ).then_inc(m_act.sig(f"PT{b}"), 1)

                def stick(b):
                    act.wait_ge(m_dve.s, m_dve.at(f"s{b}", l))
                    act.activation(att[b % 2], att[b % 2], ACT.Exp).then_inc(m_act.sig(f"a{b}"), 1)

                exps(0)
                logs(1)
                p_turned(0)
                exps(2)
                stick(1)
                p_turned(2)
                logs(3)
                stick(3)
                act.wait_ge(m_dve.s, m_dve.at("gn_var", l))
                act.activation(rstd[:, :], rstd[:, :], ACT.Sqrt).then_inc(m_act.sig("gn_sqrt"), 1)
                turn(l * 4 + 2, None)

            act.wait_ge(s_const, 16 * (len(CONSTS) + 1))
            act.activation(cvec[:, 1, :, :], cvec[:, 0, :, :], ACT.Sigmoid).then_inc(cond_sig, 1)
            act.wait_ge(zeroed, 3)
            for job in range(FIRST_JOBS):
                mod_row(job, job == 0)
            with act.Fori(0, LAYERS) as l:
                ffn(l, 0)
                norm(l * 3)
                turn(l * 4 + 1, l * 3 + 1)
                mixer(l)
                norm(l * 3 + 1)
                ffn(l, 1)
                norm(l * 3 + 2)

            turn(8, 6)
            turn(9, 7, ctx_uT)
            for t in range(TT):
                act.wait_ge(m2_pe.s, m2_pe.at(f"c{t}"))
                act.activation(ctx_kv[:, t, :], psum[:, 6 + t, 0:256], copy).then_inc(m2_act.sig(f"c{t}"), 1)
            for t in range(TT):
                for b in range(3):
                    w = 512 if b < 2 else 256
                    act.wait_ge(m2_pe.s, m2_pe.at(f"p{t}{b}"))
                    act.activation(proj2[:, t, 512 * b:512 * b + w], psum[:, 3 * t + b, 0:w], copy
                                   ).then_inc(m2_act.sig(f"p{t}{b}"), 1)
            for i in range(2):
                act.wait_ge(m2_pe.s, m2_pe.at(f"grp{i}"))
                for g in (2 * i, 2 * i + 1):
                    ins = act.activation(uT[:, 4 + g, :], psum[:, 2 + i, S * (g % 2):S * (g % 2) + S], copy, scale=p_scale[:, g:g + 1])
                ins.then_inc(m2_act.sig(f"grp{i}"), 1)
            act.wait_ge(m2_dve.s, m2_dve.at("sq"))
            act.activation(stats[:, 0:4, :], stats[:, 0:4, :], ACT.Sqrt).then_inc(m2_act.sig("rms"), 1)
            act.wait_ge(m2_pe.s, m2_pe.at("kT"))
            act.activation(kT2[:, :], psum[:, 4, :], copy).then_inc(m2_act.sig("kT"), 1)
            act.wait_ge(m2_pe.s, m2_pe.at("q"))
            for j in (2, 3):
                for g in range(2):
                    rows_ = slice(64 * g, 64 * g + 64)
                    ins = act.activation(qm[rows_, 2 * j + g, :], psum[rows_, 6, S * (j % 2):S * (j % 2) + S], copy)
            ins.then_inc(m2_act.sig("q"), 1)
            def exp2(n):
                act.wait_ge(m2_dve.s, m2_dve.at(f"max{n}"))
                act.activation(prob[:, n % 2, :], psum[:, 4 + n % 2, :], ACT.Exp, bias=key_max[:, n:n + 1], scale=HD ** -0.5,
                               accum_out=den[:, n:n + 1]).then_inc(m2_act.sig(f"e{n}"), 1)
            exp2(0)
            for n in range(16):
                if n < 15:
                    exp2(n + 1)
                act.wait_ge(m2_pe.s, m2_pe.at(f"T{n}"))
                act.activation(probT[:, n % 2, :], psum[:, 6 + n % 2, :], copy).then_inc(m2_act.sig(f"PT{n}"), 1)
            act.wait_ge(m2_pe.s, m2_pe.at("yT0"))
            act.activation(uT[:, 0:2, :], part(psum[:, 4, :], 0, 2, S), copy).then_inc(m2_act.sig("yT0"), 1)
            norm(6)

            def experts(layer):
                act.wait_ge(r_dve.s, r_dve.at("max", layer))
                for t in range(TT):
                    ins = act.activation(routeT[:, t, EXPERTS:2 * EXPERTS], psum[:, 4, EXPERTS * t:EXPERTS * t + EXPERTS], ACT.Exp,
                                         bias=neg_max[:, 0, t:t + 1], accum_out=den[:, t:t + 1])
                ins.then_inc(r_act.sig("exp"), 1)
                for kc in (0, 2, 4, 6):
                    act.wait_ge(r_pe.s, r_pe.at(f"g{kc}", layer))
                    act.activation(xeT[:, kc, :], psum[:, kc, :], copy, bias=shift_c[:, kc:kc + 1], scale=scale_c[:, kc:kc + 1]
                                   ).then_inc(r_act.sig(f"g{kc}"), 1)
                with act.Fori(0, EXPERTS) as e:
                    E = e + EXPERTS * layer
                    act.wait_ge(e_pe.s, e_pe.at("k7", E))
                    act.activation(e_silu[:, :], psum[:, 4, 0:256], ACT.Silu).then_inc(e_act.sig("silu"), 1)
                    act.wait_ge(e_pe.s, e_pe.at("hT", E))
                    act.activation(e_hT[:, :, :], part(psum[:, 5, :], 0, 4, P)[:, 0:2, :], copy).then_inc(e_act.sig("hT"), 1)
                    act.wait_ge(e_pe.s, e_pe.at("d3", E))
                    for q in range(2):
                        ins = act.activation(R[32 * q:32 * q + 32, 256 * q:256 * q + 256], psum[32 * q:32 * q + 32, 6, 0:256], copy)
                    ins.then_inc(e_act.sig("R"), 1)
            turn(10, 8)
            experts(0)
            norm(7, late=True)
            turn(11, 9)
            for fb in range(KC):
                act.wait_ge(cv_pe.s, cv_pe.at(f"f{fb}"))
                if fb >= 2:
                    act.wait_ge(cv_dve.s, cv_dve.at(f"f{fb - 2}"))
                bk = psum[:, 4 + 2 * (fb % 2), :]
                act.activation(conv_c[:, fb % 2, :], bk[:, S:2 * S], copy)
                act.activation(conv_b[:, fb % 2, :], bk[:, 0:S], copy).then_inc(cv_act.sig(f"f{fb}"), 1)
            norm(8, late=True)
            turn(12, 10)
            experts(1)
            norm(9, late=True)

        @block.vector
        def _(dve):
            mul, add, sub = ALU.mult, ALU.add, ALU.subtract

            def columns(m):
                dve.wait_ge(cols_landed, m * 32 + 32)
                dve.tensor_scalar(scale_c[:, :], scale_c[:, :], 1.0, None, add).then_inc(cols_ready, 1)
                dve.drain()

            def turn(inst, m, dst=uT, split=False):
                if m is not None:
                    columns(m)
                for b in (2, 3):
                    dve.wait_ge(tr_pe, inst * 4 + (b + 1))
                    for q in range(2):
                        kc = 2 * b + q
                        src = psum[:, 4 + b, S * q:S * q + S]
                        if m is None:
                            ins = dve.tensor_copy(dst[:, kc, :], src)
                        else:
                            for o in (dst[:, kc, :], u_hi[:, kc, :])[:1 + split]:
                                ins = dve.tensor_scalar(o, src, scale_c[:, kc:kc + 1], shift_c[:, kc:kc + 1], mul, add)
                ins.then_inc(tr_dve, 1)
                if split:
                    dve.drain()
                    dve.tensor_tensor(u_lo[:, 4:8, :], uT[:, 4:8, :], u_hi[:, 4:8, :].bitcast(F32), sub)
                    dve.wait_ge(tr_act, inst + 2)
                    dve.tensor_tensor(u_lo[:, 0:4, :], uT[:, 0:4, :], u_hi[:, 0:4, :].bitcast(F32), sub).then_inc(u_low, 1)

            def norm(p, acc, alpha, res, eps, bias=gate_row):
                dve.wait_ge(rows_landed, p * 32 + 32)
                if res is not None:
                    dve.tensor_scalar(gate_row[:, :], gate_row[:, :], 1.0, res, add, mul)
                    dve.drain()
                dve.wait_ge(*acc)
                for t in range(TT):
                    ins = dve.tensor_tensor(part(tmp[:, t, :], 0, 2, 512), psum[:, 2 * t:2 * t + 2, :], part(gate_row[:, :], 0, 2, 512), mul)
                ins.then_inc(gated, 1)
                dve.drain()
                for t in range(TT):
                    dve.scalar_tensor_tensor(tmp[:, t, :], x_tok[:, t, :], alpha, tmp[:, t, :], mul, add)
                dve.drain()
                for t in range(TT):
                    for h in range(2):
                        dve.bn_stats(stats[:, 2 * t + h, :], tmp[:, t, 512 * h:512 * h + 512])
                dve.drain()
                for t in range(TT):
                    dve.bn_aggr(mv[:, t, :], stats[:, 2 * t:2 * t + 2, :])
                dve.drain()
                dve.tensor_scalar(rstd[:, 0:TT], mv[:, 0:TT, 1], eps, None, add).then_inc(pn_var, 1)
                for t in range(TT):
                    dve.scalar_tensor_tensor(tmp[:, t, :], tmp[:, t, :], mv[:, t, 0:1], gain_row[:, :], sub, mul)
                dve.wait_ge(pn_sqrt, p + 1)
                dve.reciprocal(rstd[:, 0:TT], rstd[:, 0:TT])
                dve.drain()
                if bias is gate_row:
                    dve.wait_ge(lnb_landed, p * 16 + 16)
                else:
                    dve.wait_ge(lnb_late, (p - 6) * 16)
                for t in range(TT):
                    dve.scalar_tensor_tensor(x_tok[:, t, :], tmp[:, t, :], rstd[:, t:t + 1], bias[:, :], mul, add
                                             ).then_inc(pn_x, 1)

            def ffn(l, k):
                f0 = 1 + l * (2 * TILES) + k * TILES

                def low_gate_up(t, i=0):
                    b = 3 * ((t // 2 + k) % 2)
                    dve.wait_ge(hi_gu, f0 + i * 4 + (t + 1))
                    dve.wait_ge(pe_gu, f0 + i * 4 + (t - 1) if t else f0)
                    for g in range(2):
                        ins = dve.tensor_tensor(gu_lo[:, t % 2, g, :, :],
                                                part(W[:, b + g, :], 0, KC, STEP)[:, :, P * (t % 2):P * (t % 2) + P],
                                                gu_hi[:, t % 2, g, :, :].bitcast(F32), sub)
                    ins.then_inc(lo_gu, 1)

                def low_down(t, i=0):
                    b = 3 * ((t // 2 + k) % 2)
                    dve.wait_ge(hi_d, f0 + i * 4 + (t + 1))
                    dve.wait_ge(pe_down, f0 + i * 4 + (t - 1) if t else f0)
                    dve.tensor_tensor(d_lo[:, t % 2, :], part(W[:, b + 2, :], 0, 2, D)[:, t % 2, :],
                                      d_hi[:, t % 2, :].bitcast(F32), sub).then_inc(lo_d, 1)

                def hidden(t, i=0):
                    dve.wait_ge(act_silu, f0 + i * 4 + (t + 1))
                    if t >= 1:
                        dve.wait_ge(pe_down, f0 + i * 4 + (t - 1))
                    h_, hi, lo = h_now[:, t % 2, :], h_hi[:, t % 2, :], h_lo[:, t % 2, :]
                    dve.tensor_tensor(h_, silu_g[:, t % 2, :], psum[:, 4 + t % 2, S:2 * S], mul)
                    dve.drain()
                    dve.tensor_copy(hi, h_)
                    dve.drain()
                    dve.tensor_tensor(lo, h_, hi.bitcast(F32), sub).then_inc(dve_h, 1)
                low_gate_up(0)
                low_gate_up(1)
                turn(l * 4 + (0, 3)[k], l * 3 + 2 * k, split=True)
                low_down(0)
                hidden(0)
                with dve.Fori(0, PAIRS) as i:
                    for t in range(1, 5):
                        low_gate_up(t + 1, i)
                        low_down(t, i)
                        hidden(t, i)
                low_down(TILES - 1)
                hidden(TILES - 1)

            def rotate(l, kind, table):
                for t in range(TT):
                    if t:
                        dve.drain()
                    x = proj[:, t, QCOL[kind]:QCOL[kind] + 512]
                    x4, a4, b4 = (part(v, 0, 2 * NH, 2, 32) for v in (x, rope_a, rope_b))
                    c_, s_ = (K["rope1"][:, 2 * table + n, t, :] for n in range(2))
                    dve.tensor_tensor(a4, x4, c_.unsqueeze(1).unsqueeze(1).to_broadcast([P, 2 * NH, 2, 32]), mul)
                    s8 = s_.unsqueeze(1).to_broadcast([P, 2 * NH, 32])
                    for n in range(2):
                        dve.tensor_tensor(b4[:, :, n, :], x4[:, :, 1 - n, :], s8, mul)
                    dve.drain()
                    dve.tensor_tensor(x4[:, :, 0, :], a4[:, :, 0, :], b4[:, :, 0, :], sub)
                    ins = dve.tensor_tensor(x4[:, :, 1, :], a4[:, :, 1, :], b4[:, :, 1, :], add)
                ins.then_inc(m_dve.sig(f"rot{table}"), 1)

            def mixer(l):
                for table, (kind, group) in enumerate(((RET, 0), (DIL, 3))):
                    dve.drain()
                    dve.wait_ge(m_act.s, m_act.at(f"ev{2 * group + 1}", l))
                    rotate(l, kind, table)
                for g in (1, 3, 5):
                    kind, hb = g // 2, g % 2
                    bk = psum[:, 4 + g % 4, :]
                    dve.wait_ge(m_pe.s, m_pe.at(f"qk{g}", l))
                    for hh in range(2):
                        rows_ = slice(64 * hh, 64 * hh + 64)
                        dve.tensor_copy(qm[rows_, NH * kind + 2 * hb + hh, :], bk[rows_, 0:S])
                    dve.tensor_copy(kT[:, 2 * kind + hb, :], bk[:, S:2 * S]).then_inc(m_dve.sig(f"qk{g}"), 1)

                def pair(b):
                    return psum[:, 4 + 2 * (b % 2):6 + 2 * (b % 2), 0:3 * P]

                def both(x, n):
                    return x.unsqueeze(1).to_broadcast([P, 2, n])

                def maxima(b):
                    dve.wait_ge(m_pe.s, m_pe.at(f"A{b}", l))
                    a, closed = att[b % 2], K["closed"]
                    dve.scalar_tensor_tensor(a[:, :, 0:P], pair(b)[:, :, 0:P], HD ** -0.5, both(closed[:, P:S], P), mul, add)
                    dve.scalar_tensor_tensor(a[:, :, P:3 * P], pair(b)[:, :, P:3 * P], HD ** -0.5, both(closed[:, :], S), mul, add)
                    dve.drain()
                    m = part(neg_max[:, b // 2, :], 0, 2, 2)
                    dve.tensor_reduce(m[:, :, 0], a[:, :, 0:P], AX_X, ALU.max, negate=True)
                    dve.tensor_reduce(m[:, :, 1], a[:, :, P:3 * P], AX_X, ALU.max, negate=True).then_inc(m_dve.sig(f"max{b}"), 1)

                def weighted(b):
                    dve.wait_ge(m_act.s, m_act.at(f"exp{b}", l))
                    for hh in range(2):
                        a, d = att[b % 2][:, hh, :], den[:, 4 * (b // 2) + 2 * hh:4 * (b // 2) + 2 * hh + 2]
                        dve.scalar_tensor_tensor(a[:, 0:P], a[:, 0:P], 1.0, K["windows"][:, P:S], mul, mul, accum_out=d[:, 0:1])
                        ins = dve.scalar_tensor_tensor(a[:, P:3 * P], a[:, P:3 * P], 1.0, K["windows"][:, :], mul, mul,
                                                       accum_out=d[:, 1:2])
                    ins.then_inc(m_dve.sig(f"p{b}"), 1)

                def dil_out(b):
                    dve.wait_ge(m_pe.s, m_pe.at(f"C{b}", l))
                    d = den[:, 4 * (b // 2):4 * (b // 2) + 4]
                    dve.reciprocal(d, d)
                    dve.drain()
                    for hh in range(2):
                        for t in range(TT):
                            h = 2 * (b // 2) + hh
                            ins = dve.tensor_scalar(y_tok[:, t, 512 + HD * h:512 + HD * h + HD], psum[:, 2, S * t + HD * h:S * t + HD * h + HD],
                                                    d[:, 2 * hh + t:2 * hh + t + 1], None, mul)
                    ins.then_inc(m_dve.sig(f"y{b}"), 1)

                def neg_abs(b):
                    dve.wait_ge(m_pe.s, m_pe.at(f"A{b}", l))
                    dve.tensor_scalar(stb_z, pair(b), HD ** -0.5, None, mul)
                    dve.drain()
                    dve.scalar_tensor_tensor(stb_l, stb_z, -1.0, stb_z, mul, ALU.min).then_inc(m_dve.sig(f"na{b}"), 1)

                def mask_own(x):
                    dve.tensor_tensor(x[:, :, 0:P], x[:, :, 0:P], both(K["strict"][:, :], P), mul)
                    return dve.tensor_tensor(x[:, :, S:3 * P], x[:, :, S:3 * P], both(K["strict"][:, :], P), mul)

                def keeps(b):
                    dve.wait_ge(m_act.s, m_act.at(f"ln{b}", l))
                    dve.scalar_tensor_tensor(att[b % 2], stb_z, 0.0, stb_l, ALU.min, sub)
                    dve.drain()
                    dve.tensor_tensor(stb_z, att[b % 2], stb_z, sub)
                    dve.drain()
                    mask_own(stb_z).then_inc(m_dve.sig(f"lk{b}"), 1)

                def sticks(b):
                    dve.wait_ge(m_pe.s, m_pe.at(f"B{b}", l))
                    dve.tensor_tensor(att[b % 2], att[b % 2], pair(b), add).then_inc(m_dve.sig(f"s{b}"), 1)

                def stick_mask(b):
                    dve.wait_ge(m_act.s, m_act.at(f"a{b}", l))
                    mask_own(att[b % 2]).then_inc(m_dve.sig(f"am{b}"), 1)

                def stick_out(b):
                    dve.wait_ge(m_pe.s, m_pe.at(f"C{b}", l))
                    c = P * (b // 2)
                    dve.tensor_copy(y_tok[:, :, 768 + c:768 + c + P], part(psum[:, 3, :], 0, TT, S)[:, :, c:c + P]
                                    ).then_inc(m_dve.sig(f"y{b}"), 1)

                def decayed(b):
                    dve.wait_ge(m_pe.s, m_pe.at(f"A{b}", l))
                    h = 2 * ATT[b][1]
                    dve.tensor_tensor(att[b % 2][:, :, 0:S], pair(b)[:, :, 0:S], K["decay"][:, h:h + 2, :], mul)
                    dve.tensor_tensor(att[b % 2][:, :, S:3 * P], pair(b)[:, :, S:3 * P], K["decay"][:, h:h + 2, 0:P], mul
                                      ).then_inc(m_dve.sig(f"r{b}"), 1)

                maxima(0)
                neg_abs(1)
                weighted(0)
                keeps(1)
                maxima(2)
                dil_out(0)
                sticks(1)
                stick_mask(1)
                weighted(2)
                neg_abs(3)
                stick_out(1)
                keeps(3)
                dil_out(2)
                sticks(3)
                decayed(4)
                stick_mask(3)
                decayed(5)
                stick_out(3)
                dve.wait_ge(m_pe.s, m_pe.at("C5", l))
                for t in range(TT):
                    for h in range(NH):
                        dve.bn_stats(stats[:, NH * t + h, :], psum[:, t, RDV * h:RDV * h + RDV])
                dve.drain()
                for n in range(2 * NH):
                    dve.bn_aggr(mv[:, n, :], stats[:, n, :])
                dve.drain()
                dve.tensor_scalar(rstd[:, :], mv[:, :, 1], GN_EPS, None, add).then_inc(m_dve.sig("gn_var"), 1)
                dve.wait_ge(m_act.s, m_act.at("gn_sqrt", l))
                dve.reciprocal(rstd[:, :], rstd[:, :])
                dve.drain()
                for t in range(TT):
                    for h in range(NH):
                        n = NH * t + h
                        dve.tensor_scalar(y_tok[:, t, RDV * h:RDV * h + RDV], psum[:, t, RDV * h:RDV * h + RDV],
                                          mv[:, n, 0:1], rstd[:, n:n + 1], sub, mul)
                dve.drain()
                dve.wait_ge(m_act.s, m_act.at("silu_g", l))
                dve.tensor_tensor(y_tok[:, :, 0:512], y_tok[:, :, 0:512], proj[:, :, RG:RG + 512], mul).then_inc(m_dve.sig("y"), 1)
                turn(l * 4 + 2, None)

            for sem_ in (hi_gu, hi_d, lo_gu, lo_d, pe_gu, pe_down, act_silu, dve_h, tr_act, tr_dve):
                dve.engine_nop().then_inc(sem_, 1)
            dve.wait_ge(s_x, 16)
            dve.engine_nop().then_inc(pn_x, 2)
            dve.wait_ge(cond_sig, 1)
            dve.tensor_tensor(cvec[:, 0, :, :], cvec[:, 0, :, :], cvec[:, 1, :, :], mul)
            dve.drain()
            for n, (a, b) in enumerate(((0, MOD2), (MOD2, CTX_ROW), (CTX_ROW, JOBS))):
                dve.tensor_copy(cond[:, a:b, :], cvec[:, 0, n, :].unsqueeze(1).to_broadcast([P, b - a, KC]))
            dve.drain()
            dve.engine_nop().then_inc(cond_made, 1)
            with dve.Fori(0, LAYERS) as l:
                ffn(l, 0)
                norm(l * 3, (pe_down, l * (2 * TILES) + (1 + TILES)), ALPHA, 0.5, LN_EPS)
                turn(l * 4 + 1, l * 3 + 1)
                mixer(l)
                norm(l * 3 + 1, (m_pe.s, m_pe.at("out", l)), ALPHA, 1.0, LN_EPS)
                ffn(l, 1)
                norm(l * 3 + 2, (pe_down, l * (2 * TILES) + (1 + 2 * TILES)), ALPHA, 0.5, LN_EPS)

            turn(8, 6)
            turn(9, 7, ctx_uT)
            dve.wait_ge(s_const2, 16 * (len(CONSTS2) + 1))
            for i in range(2):
                dve.wait_ge(m2_pe.s, m2_pe.at(f"pool{i}"))
                dve.tensor_copy(pooledT[:, 2 * i:2 * i + 2, :], part(psum[:, 2 + i, :], 0, 2, S)).then_inc(m2_dve.sig(f"pool{i}"), 1)
            ms = part(stats[:, 0:4, :].rearrange("p a b -> p (a b)"), 0, TT, 12)
            for t in range(TT):
                dve.tensor_tensor(squares[:, t, 0:640], proj2[:, t, 0:640], proj2[:, t, 0:640], mul)
                dve.tensor_tensor(squares[:, t, 640:768], ctx_kv[:, t, 0:P], ctx_kv[:, t, 0:P], mul)
            dve.drain()
            for t in range(TT):
                dve.tensor_reduce(ms[:, t, :], part(squares[:, t, :], 0, 12, HD), AX_X, add)
            dve.drain()
            dve.tensor_scalar(ms, ms, 1.0 / HD, NORM_EPS, mul, add).then_inc(m2_dve.sig("sq"), 1)
            dve.wait_ge(m2_act.s, m2_act.at("rms"))
            dve.reciprocal(ms, ms)
            dve.drain()
            heads = [(part(proj2[:, t, 0:512], 0, 8, HD), t, 0, 8, 0) for t in range(TT)]
            heads += [(part(proj2[:, t, 512:640], 0, 2, HD), t, 8, 2, 1) for t in range(TT)]
            heads += [(part(ctx_kv[:, t, 0:P], 0, 2, HD), t, 10, 2, 1) for t in range(TT)]
            for x, t, h0, n, _ in heads:
                dve.tensor_tensor(x, x, ms[:, t, h0:h0 + n].unsqueeze(2).to_broadcast([P, n, HD]), mul)
            dve.drain()
            for x, _, _, n, g in heads:
                dve.tensor_tensor(x, x, qk_gain[:, g, :].unsqueeze(1).to_broadcast([P, n, HD]), mul)
            dve.drain()
            for t in range(TT):
                if t:
                    dve.drain()
                x, a, b = (part(v, 0, 10, 32, 2) for v in (proj2[:, t, 0:640], tmp[:, 0, 0:640], tmp[:, 1, 0:640]))
                c_, s_ = rope2[:, 0, t, :], rope2[:, 1, t, :]
                dve.tensor_tensor(a, x, c_.unsqueeze(1).unsqueeze(3).to_broadcast([P, 10, 32, 2]), mul)
                s10 = s_.unsqueeze(1).to_broadcast([P, 10, 32])
                for n in range(2):
                    dve.tensor_tensor(b[:, :, :, n], x[:, :, :, 1 - n], s10, mul)
                dve.drain()
                dve.tensor_tensor(x[:, :, :, 0], a[:, :, :, 0], b[:, :, :, 0], sub)
                ins = dve.tensor_tensor(x[:, :, :, 1], a[:, :, :, 1], b[:, :, :, 1], add)
            ins.then_inc(m2_dve.sig("rope"), 1)
            dve.wait_ge(m2_pe.s, m2_pe.at("q"))
            for j in (0, 1):
                for g in range(2):
                    rows_ = slice(64 * g, 64 * g + 64)
                    ins = dve.tensor_copy(qm[rows_, 2 * j + g, :], psum[rows_, 5, S * j:S * j + S])
            ins.then_inc(m2_dve.sig("q"), 1)
            for n in range(16):
                dve.wait_ge(m2_pe.s, m2_pe.at(f"S{n}"))
                dve.tensor_reduce(key_max[:, n:n + 1], psum[:, 4 + n % 2, :], AX_X, ALU.max, negate=True)
                dve.drain()
                dve.tensor_scalar(key_max[:, n:n + 1], key_max[:, n:n + 1], HD ** -0.5, None, mul).then_inc(m2_dve.sig(f"max{n}"), 1)
            dve.wait_ge(m2_pe.s, m2_pe.at("V15"))
            dve.reciprocal(den[:, :], den[:, :])
            dve.drain()
            for t in range(TT):
                d = den[:, :].rearrange("p (h t) -> p t h", t=2)[:, t, :]
                ins = dve.tensor_tensor(part(proj2[:, t, 0:512], 0, 8, HD), part(psum[:, t, :], 0, 8, HD),
                                        d.unsqueeze(2).to_broadcast([P, 8, HD]), mul)
            ins.then_inc(m2_dve.sig("y"), 1)
            dve.wait_ge(m2_pe.s, m2_pe.at("yT1"))
            dve.tensor_copy(uT[:, 2:4, :], part(psum[:, 5, :], 0, 2, S)).then_inc(m2_dve.sig("yT1"), 1)
            norm(6, (m2_pe.s, m2_pe.at("out")), ALPHA, None, NORM_EPS)

            def experts(layer):
                X = slice(0, EXPERTS)
                dve.wait_ge(r_pe.s, r_pe.at("logits", layer))
                dve.tensor_reduce(neg_max[:, 0, 0:TT], part(psum[:, 4, :], 0, 32, EXPERTS)[:, 0:TT, :], AX_X, ALU.max, negate=True
                                  ).then_inc(r_dve.sig("max"), 1)
                dve.memset(R[:, :], 0.0)
                dve.wait_ge(r_act.s, r_act.at("exp", layer))
                dve.reciprocal(den[:, 0:TT], den[:, 0:TT])
                dve.drain()
                gates = routeT[:, :, EXPERTS:2 * EXPERTS]
                dve.tensor_tensor(gates, gates, den[:, 0:TT].unsqueeze(2).to_broadcast([P, TT, EXPERTS]), mul
                                  ).then_inc(r_dve.sig("aff"), 1)
                dve.wait_ge(r_pe.s, r_pe.at("affT", layer))
                dve.tensor_copy(route[X, 0, :], psum[X, 5, 0:S])
                dve.drain()
                src, dst = route[X, 0, :], route[X, 1, :]
                for r in range(CAP // 8):
                    dve.max(top8[X, :], src)
                    dve.drain()
                    dve.match_replace(dst, top8[X, :], src, -1.0)
                    dve.drain()
                    src, dst = dst, route[X, 1 + (r + 1) % 2, :]
                dve.tensor_scalar(route[X, 1, :], src, 0.0, None, ALU.is_lt)
                dve.drain()
                dve.tensor_tensor_scan(route[X, 3, :], route[X, 1, :], route[X, 1, :], 0.0, add, ALU.max)
                dve.drain()
                dve.tensor_tensor(route[X, 3, :], route[X, 3, :], route[X, 1, :], mul).then_inc(r_dve.sig("slot"), 1)
                dve.wait_ge(r_pe.s, r_pe.at("slotT", layer))
                dve.tensor_copy(routeT[:, :, 0:EXPERTS], part(psum[:, 5, :], 0, 32, EXPERTS)[:, 0:TT, :])
                dve.drain()
                for t in range(TT):
                    ins = dve.tensor_tensor(part(sel[:, t, :], 0, EXPERTS, CAP), routeT[:, t, X].unsqueeze(2).to_broadcast([P, EXPERTS, CAP]),
                                            slot_no[:, 0:CAP].unsqueeze(1).to_broadcast([P, EXPERTS, CAP]), ALU.is_equal)
                ins.then_inc(r_dve.sig("sel"), 1)
                for kc in (1, 3, 5, 7):
                    dve.wait_ge(r_pe.s, r_pe.at(f"g{kc}", layer))
                    dve.tensor_scalar(xeT[:, kc, :], psum[:, kc, :], scale_c[:, kc:kc + 1], shift_c[:, kc:kc + 1], mul, add
                                      ).then_inc(r_dve.sig(f"g{kc}"), 1)
                dve.wait_ge(r_act.s, r_act.at("g6", layer))
                dve.drain()
                with dve.Fori(0, EXPERTS) as e:
                    E = e + EXPERTS * layer
                    dve.tensor_copy(xe_now[:, :, :], xeT[:, :, ds(e * CAP, CAP)])
                    for t in range(TT):
                        ins = dve.tensor_scalar(G_now[:, t, :], slot_no[:, :], routeT[:, t, ds(e, 1)], routeT[:, t, ds(e + EXPERTS, 1)],
                                                ALU.is_equal, mul)
                    ins.then_inc(e_dve.sig("xG"), 1)
                    dve.wait_ge(e_act.s, e_act.at("silu", E))
                    dve.tensor_tensor(e_h[:, :], e_silu[:, :], psum[:, 4, 256:512], mul).then_inc(e_dve.sig("h"), 1)
                    dve.wait_ge(e_pe.s, e_pe.at("gT", E))
                    dve.tensor_copy(GT[:, :], psum[:, 7, 0:S]).then_inc(e_dve.sig("gT"), 1)
                    dve.wait_ge(e_pe.s, e_pe.at("d3", E))
                    for q in (2, 3):
                        ins = dve.tensor_copy(R[32 * q:32 * q + 32, 256 * q:256 * q + 256], psum[32 * q:32 * q + 32, 6, 0:256])
                    ins.then_inc(e_dve.sig("R"), 1)
            turn(10, 8)
            experts(0)
            norm(7, (e_pe.s, e_pe.at("out", EXPERTS - 1)), ALPHA, None, NORM_EPS, bias_late)
            turn(11, 9)
            dve.memset(conv_s[:, :, 0:S + 2:S + 1], 0.0)
            dve.drain()
            for fb in range(KC):
                q = fb % 2
                dve.wait_ge(cv_act.s, cv_act.at(f"f{fb}"))
                dve.tensor_tensor(conv_s[:, q, 1:S + 1], conv_c[:, q, :], psum[:, 5 + 2 * q, 0:S], mul)
                dve.drain()
                dve.tensor_scalar(conv_z[:, q, :], conv_s[:, q, 0:S], conv_w[:, fb, 0:1], None, mul)
                for j in (1, 2):
                    dve.drain()
                    dve.scalar_tensor_tensor(conv_z[:, q, :], conv_s[:, q, j:j + S], conv_w[:, fb, j:j + 1], conv_z[:, q, :], mul, add)
                dve.drain()
                dve.tensor_tensor(conv_yT[:, fb, :], conv_z[:, q, :], conv_b[:, q, :], mul).then_inc(cv_dve.sig(f"f{fb}"), 1)
            norm(8, (cv_pe.s, cv_pe.at("out")), ALPHA, None, NORM_EPS, bias_late)
            turn(12, 10)
            experts(1)
            norm(9, (e_pe.s, e_pe.at("out", 2 * EXPERTS - 1)), ALPHA, None, NORM_EPS, bias_late)


def kernel(**inputs):
    import concourse.bacc as bacc
    from concourse.bass_utils import run_bass_kernel_spmd as run

    def cols(v):
        v = np.asarray(v)
        return np.ascontiguousarray(np.moveaxis(v.reshape(v.shape[:-1] + (KC, P)), -1, 0))
    g = {k: np.asarray(v) for k, v in inputs.items()}
    a = {n: g[n] for n in ("ffn1_w_gate", "ffn1_w_up", "ffn1_w_down", "w_in", "w_out",
                           "ffn2_w_gate", "ffn2_w_up", "ffn2_w_down")}
    a["x"], a["ctx"] = g["x"][0], g["ctx_2"][0]
    q_cols = np.arange(QH * HD).reshape(2, QH // 2, HD).transpose(1, 0, 2).ravel()
    a["w_mix_in"] = g["w_mix_in_2"][0][:, np.concatenate([q_cols, np.arange(QH * HD, MIX2_W)])]
    a["w_mix_out"] = g["w_mix_out_2"][0]
    a["w_conv_in"], a["w_conv_out"] = g["w_conv_in_2"][0], g["w_conv_out_2"][0]
    a["w_exp_gate"], a["w_exp_up"], a["w_exp_down"] = g["w_exp_gate_2"], g["w_exp_up_2"], g["w_exp_down_2"]
    ada = g["w_ada"].reshape(LAYERS, D, 9, D).transpose(0, 2, 1, 3).reshape(MOD2, D, D)
    mod = g["w_mod_2"].reshape(LAYERS, D, 6, D).transpose(0, 2, 1, 3).reshape(12, D, D)
    a["mod_w"] = np.concatenate([ada, mod, mod[0:2]])
    mod_b = g["b_mod_2"].reshape(12, D)
    a["mod_b"] = np.concatenate([g["b_ada"].reshape(MOD2, D), mod_b, mod_b[0:2]])
    a["cvec"] = cols(np.stack([g["c"][0], g["c_2"][0], g["c_ctx_2"]]))
    a["ln_g"] = np.concatenate([g["ln_gain"].reshape(6, D), np.stack([g["ln_mix_g_2"], g["ln_ffn_g_2"]], 1).reshape(4, D)])
    a["ln_b"] = np.concatenate([g["ln_bias"].reshape(6, D), np.stack([g["ln_mix_b_2"], g["ln_ffn_b_2"]], 1).reshape(4, D)])
    a["w_grp"] = g["w_pool_grp_2"][0].transpose(1, 0, 2)
    a["qk_gain"] = np.tile(np.stack([g["q_norm_g_2"][0], g["k_norm_g_2"][0]])[None], (P, 1, 1))
    a["p_scale"] = g["pool_scale_2"][0].reshape(4, P).T
    a["w_router"] = g["w_router_2"].reshape(LAYERS, KC, P, EXPERTS).transpose(2, 0, 1, 3).reshape(P, LAYERS, KC * EXPERTS)
    a["conv_w"] = g["conv_w_2"][0].reshape(3, KC, P).transpose(2, 1, 0)
    a.update(stack_constants())
    a = {"in_" + k: np.ascontiguousarray(v) for k, v in a.items()}

    nc = bacc.Bacc("TRN2", target_bir_lowering=False, num_devices=1)
    aps = {k[3:]: nc.dram_tensor(k, v.shape, mybir.dt.from_np(v.dtype), kind="ExternalInput").ap() for k, v in a.items()}
    out = nc.dram_tensor("out", (S, D), F32, kind="ExternalOutput").ap()
    build(nc, aps, out)
    r = run(nc, [a], core_ids=[0])
    return r.results[0]["out"].reshape(1, S, D)
```
